# Optimizing a Trainium2 kernel written in Bass

```python
import math
import jax
import jax.numpy as jnp
from jax import lax
import numpy as np
import jax, jax.numpy as jnp

D_MODEL = 2048
BATCH = 1
SEQ = 256
DEPTH = 1

CTX_LEN = 256
GRID_W = 64
N_DIR = 2
D_MIX = D_MODEL
SSD_WIDTH = D_MIX // 2
GDN_WIDTH = D_MIX - SSD_WIDTH
SSD_HEAD_DIM = 64
SSD_HEADS = SSD_WIDTH // SSD_HEAD_DIM
SSD_GROUPS = 2
SSD_HEADS_PER_GROUP = SSD_HEADS // SSD_GROUPS
SSD_STATE = 128
SSD_CONV_DIM = SSD_WIDTH + 2 * SSD_GROUPS * SSD_STATE
GDN_HEAD_DIM = 128
GDN_HEADS = GDN_WIDTH // GDN_HEAD_DIM
GDN_CONV_DIM = 3 * GDN_WIDTH
CONV_K = 5
CHUNK = 128
EPS = 1e-6

OFF_XBC = D_MIX
OFF_DT = OFF_XBC + SSD_CONV_DIM
OFF_QKV = OFF_DT + N_DIR * SSD_HEADS
OFF_BETA = OFF_QKV + GDN_CONV_DIM
OFF_ALPHA = OFF_BETA + N_DIR * GDN_HEADS
IN_DIM = OFF_ALPHA + N_DIR * GDN_HEADS


def rms_norm(x, w):
    xf = x.astype(jnp.float32)
    y = xf * lax.rsqrt(jnp.mean(xf * xf, axis=-1, keepdims=True) + EPS)
    return (y * w.astype(jnp.float32)).astype(x.dtype)

def l2_norm(t):
    return t * lax.rsqrt(jnp.sum(t * t, axis=-1, keepdims=True) + EPS)

def _flip(t):
    return t[:, ::-1]

def _same(t):
    return t

def centred_dwconv(x, w):
    pad = CONV_K // 2
    L = x.shape[1]
    xp = jnp.pad(x, ((0, 0), (pad, pad), (0, 0)))
    out = xp[:, 0:L] * w[0]
    for k in range(1, CONV_K):
        out = out + xp[:, k:k + L] * w[k]
    return out

def conv_latent(x, w):
    bsz, L, ch = x.shape
    rows = L // GRID_W
    y = centred_dwconv(x.reshape(bsz * rows, GRID_W, ch), w)
    return y.reshape(bsz, L, ch)

def _chunks(t):
    return t.reshape(t.shape[0], t.shape[1] // CHUNK, CHUNK, *t.shape[2:])

def ssd_scan(xs, dt, a_neg, bm, cm, h0):
    loga = _chunks(dt * a_neg)
    xdt = _chunks(xs * dt[..., None])
    bmc, cmc = _chunks(bm), _chunks(cm)
    acum = jnp.cumsum(loga, axis=2)
    causal = jnp.tril(jnp.ones((CHUNK, CHUNK), bool))
    a_t = jnp.moveaxis(acum, 2, -1)
    seg = a_t[..., :, None] - a_t[..., None, :]
    lmat = jnp.exp(jnp.where(causal, seg, -jnp.inf))
    cb = jnp.einsum('bcqgn,bcsgn->bcgqs', cmc, bmc)
    y_diag = jnp.einsum('bcgrqs,bcsgrp->bcqgrp', cb[:, :, :, None] * lmat, xdt)
    decay_end = jnp.exp(acum[:, :, -1:] - acum)
    states = jnp.einsum('bcsgn,bcsgrp->bcgrpn', bmc, xdt * decay_end[..., None])
    chunk_decay = jnp.exp(acum[:, :, -1])

    def step(h, inp):
        st, dec = inp
        return h * dec[..., None, None] + st, h

    h_last, h_prev = lax.scan(step, h0, (jnp.moveaxis(states, 1, 0), jnp.moveaxis(chunk_decay, 1, 0)))
    h_prev = jnp.moveaxis(h_prev, 0, 1)
    y_off = jnp.einsum('bcqgn,bcgrpn->bcqgrp', cmc, h_prev) * jnp.exp(acum)[..., None]
    return (y_diag + y_off).reshape(xs.shape), h_last

def gdn_scan(q, k, v, g, beta, s0):
    bsz, L, H, V = v.shape

    def heads_first(t):
        return jnp.moveaxis(_chunks(t), 3, 1)

    q, k, v, g, beta = (heads_first(t) for t in (q, k, v, g, beta))
    gcum = jnp.cumsum(g, axis=-1)
    incl = jnp.tril(jnp.ones((CHUNK, CHUNK), bool))
    strict = jnp.tril(jnp.ones((CHUNK, CHUNK), bool), -1)
    decay = jnp.exp(jnp.where(incl, gcum[..., :, None] - gcum[..., None, :], -jnp.inf))
    k_beta = k * beta[..., None]
    a_strict = jnp.where(strict, jnp.einsum('bhcik,bhcjk->bhcij', k_beta, k) * decay, 0.0)
    rhs = jnp.concatenate([v * beta[..., None], k_beta * jnp.exp(gcum)[..., None]], axis=-1)
    sol = lax.linalg.triangular_solve(a_strict, rhs, left_side=True, lower=True, unit_diagonal=True)
    u, w = sol[..., :V], sol[..., V:]
    attn = jnp.einsum('bhcik,bhcjk->bhcij', q, k) * decay
    q_dec = q * jnp.exp(gcum)[..., None]
    k_end = k * jnp.exp(gcum[..., -1:] - gcum)[..., None]
    chunk_decay = jnp.exp(gcum[..., -1])

    def step(S, inp):
        qd, ke, ui, wi, ai, dec = inp
        v_new = ui - jnp.einsum('bhqk,bhkv->bhqv', wi, S)
        o = jnp.einsum('bhqk,bhkv->bhqv', qd, S) + jnp.einsum('bhqs,bhsv->bhqv', ai, v_new)
        S = S * dec[..., None, None] + jnp.einsum('bhsk,bhsv->bhkv', ke, v_new)
        return S, o

    xs = tuple(jnp.moveaxis(t, 2, 0) for t in (q_dec, k_end, u, w, attn, chunk_decay))
    s_last, o = lax.scan(step, s0, xs)
    o = jnp.moveaxis(jnp.moveaxis(o, 0, 2), 1, 3).reshape(bsz, L, H, V)
    return o, s_last

def ssd_mixer(xbc_c, dt_c, xbc_l, dt_l, a_log, dt_bias, d_skip):
    G, R, P, N = SSD_GROUPS, SSD_HEADS_PER_GROUP, SSD_HEAD_DIM, SSD_STATE
    a_neg = -jnp.exp(a_log.astype(jnp.float32)).reshape(N_DIR, G, R)
    bias = dt_bias.astype(jnp.float32).reshape(N_DIR, G, R)

    def unpack(xbc, dt_raw):
        bsz, L = xbc.shape[:2]
        xbc = xbc.astype(jnp.float32)
        xs = xbc[..., :SSD_WIDTH].reshape(bsz, L, G, R, P)
        bm = xbc[..., SSD_WIDTH:SSD_WIDTH + G * N].reshape(bsz, L, G, N)
        cm = xbc[..., SSD_WIDTH + G * N:].reshape(bsz, L, G, N)
        dt = jax.nn.softplus(dt_raw.astype(jnp.float32).reshape(bsz, L, N_DIR, G, R) + bias)
        return xs, bm, cm, dt

    xc, bc, cc, dtc = unpack(xbc_c, dt_c)
    xl, bl, cl, dtl = unpack(xbc_l, dt_l)
    dsk = d_skip.astype(jnp.float32).reshape(G, R)[..., None]
    y_c, y_l = xc * dsk, xl * dsk
    h0 = jnp.zeros((xc.shape[0], G, R, P, N), jnp.float32)
    for d in range(N_DIR):
        f = _flip if d else _same
        yc_d, h_ctx = ssd_scan(f(xc), f(dtc[:, :, d]), a_neg[d], f(bc), f(cc), h0)
        yl_d, _ = ssd_scan(f(xl), f(dtl[:, :, d]), a_neg[d], f(bl), f(cl), h_ctx)
        y_c = y_c + f(yc_d)
        y_l = y_l + f(yl_d)
    return y_c.reshape(*xc.shape[:2], SSD_WIDTH), y_l.reshape(*xl.shape[:2], SSD_WIDTH)

def gdn_mixer(qkv_c, b_c, a_c, qkv_l, b_l, a_l, a_log, dt_bias):
    H, K = GDN_HEADS, GDN_HEAD_DIM
    rate = jnp.exp(a_log.astype(jnp.float32))
    bias = dt_bias.astype(jnp.float32)

    def unpack(qkv, b_raw, a_raw):
        bsz, L = qkv.shape[:2]
        qkv = qkv.astype(jnp.float32).reshape(bsz, L, 3, H, K)
        q = l2_norm(qkv[:, :, 0]) * (K ** -0.5)
        k = l2_norm(qkv[:, :, 1])
        v = qkv[:, :, 2]
        beta = jax.nn.sigmoid(b_raw.astype(jnp.float32).reshape(bsz, L, N_DIR, H))
        g = -rate * jax.nn.softplus(a_raw.astype(jnp.float32).reshape(bsz, L, N_DIR, H) + bias)
        return q, k, v, beta, g

    qc, kc, vc, bec, gc = unpack(qkv_c, b_c, a_c)
    ql, kl, vl, bel, gl = unpack(qkv_l, b_l, a_l)
    s0 = jnp.zeros((qc.shape[0], H, K, K), jnp.float32)
    o_c = jnp.zeros_like(vc)
    o_l = jnp.zeros_like(vl)
    for d in range(N_DIR):
        f = _flip if d else _same
        oc_d, s_ctx = gdn_scan(f(qc), f(kc), f(vc), f(gc[:, :, d]), f(bec[:, :, d]), s0)
        ol_d, _ = gdn_scan(f(ql), f(kl), f(vl), f(gl[:, :, d]), f(bel[:, :, d]), s_ctx)
        o_c = o_c + f(oc_d)
        o_l = o_l + f(ol_d)
    return o_c, o_l

def ssd_out_norm(y, z, w):
    bsz, L = y.shape[:2]
    yg = (y * jax.nn.silu(z.astype(jnp.float32))).reshape(bsz, L, SSD_GROUPS, SSD_WIDTH // SSD_GROUPS)
    yg = yg * lax.rsqrt(jnp.mean(yg * yg, axis=-1, keepdims=True) + EPS)
    return yg.reshape(bsz, L, SSD_WIDTH) * w.astype(jnp.float32)

def gdn_out_norm(o, z, w):
    bsz, L = o.shape[:2]
    o = o * lax.rsqrt(jnp.mean(o * o, axis=-1, keepdims=True) + EPS) * w.astype(jnp.float32)
    return o.reshape(bsz, L, GDN_WIDTH) * jax.nn.silu(z.astype(jnp.float32))

def _split_proj(p):
    return (p[..., :OFF_XBC], p[..., OFF_XBC:OFF_DT], p[..., OFF_DT:OFF_QKV],
            p[..., OFF_QKV:OFF_BETA], p[..., OFF_BETA:OFF_ALPHA], p[..., OFF_ALPHA:IN_DIM])

def hybrid_layer(h_lat, h_ctx, mod_lat, mod_ctx, pre_w, post_w, w_in, conv_ssd_w, conv_ssd_b,
                 conv_gdn_w, ssd_a_log, ssd_dt_bias, ssd_d, ssd_norm_w, gdn_a_log, gdn_dt_bias,
                 gdn_norm_w, w_out, update_ctx):
    shift_l, scale_l, gate_l = jnp.split(mod_lat, 3, axis=-1)
    shift_c, scale_c, gate_c = jnp.split(mod_ctx, 3, axis=-1)
    u_l = rms_norm(h_lat, pre_w) * (1 + scale_l[:, None]) + shift_l[:, None]
    u_c = rms_norm(h_ctx, pre_w) * (1 + scale_c) + shift_c
    z_l, xbc_l, dt_l, qkv_l, b_l, a_l = _split_proj(u_l @ w_in)
    z_c, xbc_c, dt_c, qkv_c, b_c, a_c = _split_proj(u_c @ w_in)
    xbc_l = jax.nn.silu(conv_latent(xbc_l, conv_ssd_w) + conv_ssd_b)
    xbc_c = jax.nn.silu(centred_dwconv(xbc_c, conv_ssd_w) + conv_ssd_b)
    qkv_l = jax.nn.silu(conv_latent(qkv_l, conv_gdn_w))
    qkv_c = jax.nn.silu(centred_dwconv(qkv_c, conv_gdn_w))
    ssd_c, ssd_l = ssd_mixer(xbc_c, dt_c, xbc_l, dt_l, ssd_a_log, ssd_dt_bias, ssd_d)
    gdn_c, gdn_l = gdn_mixer(qkv_c, b_c, a_c, qkv_l, b_l, a_l, gdn_a_log, gdn_dt_bias)

    def merge(ssd_y, gdn_o, z, dtype):
        y = jnp.concatenate([ssd_out_norm(ssd_y, z[..., :SSD_WIDTH], ssd_norm_w),
                             gdn_out_norm(gdn_o, z[..., SSD_WIDTH:], gdn_norm_w)], axis=-1)
        return rms_norm(y.astype(dtype) @ w_out, post_w)

    h_lat = h_lat + gate_l[:, None] * merge(ssd_l, gdn_l, z_l, h_lat.dtype)
    if update_ctx:
        h_ctx = h_ctx + gate_c * merge(ssd_c, gdn_c, z_c, h_ctx.dtype)
    return h_lat, h_ctx

def _dt_bias_init(key, shape):
    dt = jnp.exp(jax.random.uniform(key, shape, jnp.float32, math.log(1e-3), math.log(1e-1)))
    return dt + jnp.log(-jnp.expm1(-dt))

def first_inputs(seed: int = 0) -> dict:
    key = jax.random.key(seed)
    ks = jax.random.split(key, 20)
    f32 = jnp.float32

    def nrm(k, shape, s):
        return jax.random.normal(k, shape, f32) * s

    return {
        'x': nrm(ks[0], (BATCH, SEQ, D_MODEL), 1.0),
        'c': nrm(ks[1], (BATCH, D_MODEL), 1.0),
        'ctx': nrm(ks[2], (BATCH, CTX_LEN, D_MODEL), 1.0),
        'c_ctx': nrm(ks[3], (D_MODEL,), 1.0),
        'w_ada': nrm(ks[4], (DEPTH, D_MODEL, 3 * D_MODEL), 0.5 * D_MODEL ** -0.5),
        'b_ada': nrm(ks[5], (DEPTH, 3 * D_MODEL), 0.01),
        'pre_norm_w': 1.0 + nrm(ks[6], (DEPTH, D_MODEL), 0.05),
        'post_norm_w': 1.0 + nrm(ks[7], (DEPTH, D_MODEL), 0.05),
        'w_in': nrm(ks[8], (DEPTH, D_MODEL, IN_DIM), D_MODEL ** -0.5),
        'conv_ssd_w': nrm(ks[9], (DEPTH, CONV_K, SSD_CONV_DIM), CONV_K ** -0.5),
        'conv_ssd_b': nrm(ks[10], (DEPTH, SSD_CONV_DIM), 0.02),
        'conv_gdn_w': nrm(ks[11], (DEPTH, CONV_K, GDN_CONV_DIM), CONV_K ** -0.5),
        'ssd_a_log': jnp.log(jax.random.uniform(ks[12], (DEPTH, N_DIR, SSD_HEADS), f32, 1.0, 16.0)),
        'ssd_dt_bias': _dt_bias_init(ks[13], (DEPTH, N_DIR, SSD_HEADS)),
        'ssd_d': 1.0 + nrm(ks[14], (DEPTH, SSD_HEADS), 0.1),
        'ssd_norm_w': 1.0 + nrm(ks[15], (DEPTH, SSD_WIDTH), 0.05),
        'gdn_a_log': jnp.log(jax.random.uniform(ks[16], (DEPTH, N_DIR, GDN_HEADS), f32, 1.0, 16.0)),
        'gdn_dt_bias': _dt_bias_init(ks[17], (DEPTH, N_DIR, GDN_HEADS)),
        'gdn_norm_w': 1.0 + nrm(ks[18], (DEPTH, GDN_HEAD_DIM), 0.05),
        'w_out': nrm(ks[19], (DEPTH, D_MIX, D_MODEL), D_MIX ** -0.5),
    }

def first_block(x, c, ctx, c_ctx, w_ada, b_ada, pre_norm_w, post_norm_w, w_in, conv_ssd_w, conv_ssd_b,
              conv_gdn_w, ssd_a_log, ssd_dt_bias, ssd_d, ssd_norm_w, gdn_a_log, gdn_dt_bias,
              gdn_norm_w, w_out):
    h_lat, h_ctx = x, ctx
    c_act = jax.nn.silu(c)
    cc_act = jax.nn.silu(c_ctx)
    for l in range(DEPTH):
        mod_lat = c_act @ w_ada[l] + b_ada[l]
        mod_ctx = cc_act @ w_ada[l] + b_ada[l]
        h_lat, h_ctx = hybrid_layer(
            h_lat, h_ctx, mod_lat, mod_ctx, pre_norm_w[l], post_norm_w[l], w_in[l],
            conv_ssd_w[l], conv_ssd_b[l], conv_gdn_w[l], ssd_a_log[l], ssd_dt_bias[l], ssd_d[l],
            ssd_norm_w[l], gdn_a_log[l], gdn_dt_bias[l], gdn_norm_w[l], w_out[l],
            update_ctx=(l < DEPTH - 1))
    return h_lat


DEPTH_2 = 2

ATTN_WIDTH = D_MODEL // 2
CONV_WIDTH = D_MODEL - ATTN_WIDTH
N_HEADS = 8
HEAD_DV = ATTN_WIDTH // N_HEADS
HEAD_DK = HEAD_DV // 2
N_CONV_GROUPS = 8
CONV_K_2 = 3
D_FF = 4 * D_MODEL
NUM_BUCKETS = 32
MAX_DISTANCE = 128
MAX_EXACT = NUM_BUCKETS // 2
Q_BLOCK = 128
NEG = -1e30
PROJ_WIDTH = 3 * ATTN_WIDTH + 3 * CONV_WIDTH


def _rmsnorm(x, g):
    x32 = x.astype(jnp.float32)
    y = x32 * lax.rsqrt(jnp.mean(x32 * x32, axis=-1, keepdims=True) + EPS)
    return (y * g.astype(jnp.float32)).astype(x.dtype)

def _relative_bucket(dist):
    n = jnp.maximum(dist, 0)
    is_small = n < MAX_EXACT
    nf = jnp.maximum(n, MAX_EXACT).astype(jnp.float32)
    large = MAX_EXACT + (jnp.log(nf / MAX_EXACT) / math.log(MAX_DISTANCE / MAX_EXACT)
                         * (NUM_BUCKETS - MAX_EXACT)).astype(jnp.int32)
    large = jnp.minimum(large, NUM_BUCKETS - 1)
    return jnp.where(is_small, n, large)

def _diff_attention(q, k, v, lam, rel_bias):
    B, S, H, _, dk = q.shape
    dv = v.shape[-1]
    nblk = S // Q_BLOCK
    k_pos = jnp.arange(S, dtype=jnp.int32)
    scale = dk ** -0.5

    def block(args):
        qb, start = args
        q_pos = start + jnp.arange(Q_BLOCK, dtype=jnp.int32)
        dist = q_pos[:, None] - k_pos[None, :]
        bias = jnp.take(rel_bias, _relative_bucket(dist), axis=0)
        bias = bias.reshape(Q_BLOCK, S, H, 2).transpose(2, 3, 0, 1).astype(jnp.float32)
        s = jnp.einsum('bqhmd,bkhmd->bhmqk', qb, k).astype(jnp.float32) * scale + bias
        s = jnp.where(dist >= 0, s, NEG)
        p = jax.nn.softmax(s, axis=-1)
        p = p[:, :, 0] - lam * p[:, :, 1]
        return jnp.einsum('bhqk,bkhd->bqhd', p.astype(v.dtype), v)

    qb = q.reshape(B, nblk, Q_BLOCK, H, 2, dk).transpose(1, 0, 2, 3, 4, 5)
    starts = jnp.arange(nblk, dtype=jnp.int32) * Q_BLOCK
    out = lax.map(block, (qb, starts))
    return out.transpose(1, 0, 2, 3, 4).reshape(B, S, H, dv)

def _short_conv(u, w):
    S = u.shape[1]
    up = jnp.pad(u, ((0, 0), (CONV_K_2 - 1, 0), (0, 0)))
    return sum(w[i] * up[:, i:i + S] for i in range(CONV_K_2))

def second_inputs(seed: int = 0) -> dict:
    key = jax.random.key(seed)
    ks = jax.random.split(key, 16)
    f32 = jnp.float32

    def nrm(k, shape, scale):
        return jax.random.normal(k, shape, f32) * scale

    def gain(k, shape):
        return 1.0 + 0.02 * jax.random.normal(k, shape, f32)

    return {
        "x": nrm(ks[0], (BATCH, SEQ, D_MODEL), 1.0),
        "w_in": nrm(ks[1], (DEPTH_2, D_MODEL, PROJ_WIDTH), D_MODEL ** -0.5),
        "w_out": nrm(ks[2], (DEPTH_2, ATTN_WIDTH + CONV_WIDTH, D_MODEL), (ATTN_WIDTH + CONV_WIDTH) ** -0.5),
        "conv_w": nrm(ks[3], (DEPTH_2, CONV_K_2, CONV_WIDTH), CONV_K_2 ** -0.5),
        "q_norm_g": gain(ks[4], (DEPTH_2, HEAD_DK)),
        "k_norm_g": gain(ks[5], (DEPTH_2, HEAD_DK)),
        "lambda_q1": nrm(ks[6], (DEPTH_2, HEAD_DK), 0.1),
        "lambda_k1": nrm(ks[7], (DEPTH_2, HEAD_DK), 0.1),
        "lambda_q2": nrm(ks[8], (DEPTH_2, HEAD_DK), 0.1),
        "lambda_k2": nrm(ks[9], (DEPTH_2, HEAD_DK), 0.1),
        "subln_g": gain(ks[10], (DEPTH_2, HEAD_DV)),
        "attn_norm_g": gain(ks[11], (DEPTH_2, D_MODEL)),
        "mlp_norm_g": gain(ks[12], (DEPTH_2, D_MODEL)),
        "w_up": nrm(ks[13], (DEPTH_2, D_MODEL, D_FF), D_MODEL ** -0.5),
        "w_down": nrm(ks[14], (DEPTH_2, D_FF, D_MODEL), D_FF ** -0.5),
        "rel_bias": nrm(ks[15], (NUM_BUCKETS, 2 * N_HEADS), 0.5),
    }

def second_block(x, w_in, w_out, conv_w, q_norm_g, k_norm_g, lambda_q1, lambda_k1,
              lambda_q2, lambda_k2, subln_g, attn_norm_g, mlp_norm_g, w_up, w_down,
              rel_bias):
    B, S, _ = x.shape
    splits = [ATTN_WIDTH, 2 * ATTN_WIDTH, 3 * ATTN_WIDTH,
              3 * ATTN_WIDTH + CONV_WIDTH, 3 * ATTN_WIDTH + 2 * CONV_WIDTH]
    for l in range(DEPTH_2):
        h = _rmsnorm(x, attn_norm_g[l])
        proj = h @ w_in[l]
        q, k, v, gate_b, gate_c, conv_in = jnp.split(proj, splits, axis=-1)

        q = _rmsnorm(q.reshape(B, S, N_HEADS, 2, HEAD_DK), q_norm_g[l])
        k = _rmsnorm(k.reshape(B, S, N_HEADS, 2, HEAD_DK), k_norm_g[l])
        v = v.reshape(B, S, N_HEADS, HEAD_DV)
        lam_init = 0.8 - 0.6 * math.exp(-0.3 * l)
        lam = (jnp.exp(jnp.sum(lambda_q1[l].astype(jnp.float32) * lambda_k1[l].astype(jnp.float32)))
               - jnp.exp(jnp.sum(lambda_q2[l].astype(jnp.float32) * lambda_k2[l].astype(jnp.float32)))
               + lam_init)
        attn = _diff_attention(q, k, v, lam, rel_bias)
        attn = (_rmsnorm(attn, subln_g[l]) * (1.0 - lam_init)).reshape(B, S, ATTN_WIDTH)

        conv = gate_b * _short_conv(gate_c * conv_in, conv_w[l])

        x = x + jnp.concatenate([attn, conv.astype(attn.dtype)], axis=-1) @ w_out[l]

        hm = _rmsnorm(x, mlp_norm_g[l]) @ w_up[l]
        x = x + jnp.square(jax.nn.relu(hm)) @ w_down[l]
    return x


def setup_inputs(seed=0):
    out = dict(first_inputs(seed))
    for name, value in second_inputs(seed + 1).items():
        if name != "x":
            out[name + "_2"] = value
    return out


def reference(
    x, c, ctx, c_ctx, w_ada, b_ada, pre_norm_w, post_norm_w, w_in, conv_ssd_w, conv_ssd_b,
    conv_gdn_w, ssd_a_log, ssd_dt_bias, ssd_d, ssd_norm_w, gdn_a_log, gdn_dt_bias, gdn_norm_w,
    w_out, w_in_2, w_out_2, conv_w_2, q_norm_g_2, k_norm_g_2, lambda_q1_2, lambda_k1_2,
    lambda_q2_2, lambda_k2_2, subln_g_2, attn_norm_g_2, mlp_norm_g_2, w_up_2, w_down_2,
    rel_bias_2,
):
    x = first_block(
        x, c, ctx, c_ctx, w_ada, b_ada, pre_norm_w, post_norm_w, w_in, conv_ssd_w, conv_ssd_b,
        conv_gdn_w, ssd_a_log, ssd_dt_bias, ssd_d, ssd_norm_w, gdn_a_log, gdn_dt_bias,
        gdn_norm_w, w_out,
    )
    return second_block(
        x, w_in_2, w_out_2, conv_w_2, q_norm_g_2, k_norm_g_2, lambda_q1_2, lambda_k1_2,
        lambda_q2_2, lambda_k2_2, subln_g_2, attn_norm_g_2, mlp_norm_g_2, w_up_2, w_down_2,
        rel_bias_2,
    )


_drawn_inputs = setup_inputs


def setup_inputs(seed=0):
    import zlib

    import numpy as np

    out = dict(_drawn_inputs(seed))
    spreads = {}
    factors = {'conv_ssd_b': 4.064,
     'ssd_d': 2.739,
     'gdn_norm_w': 3.864,
     'q_norm_g_2': 7.083,
     'k_norm_g_2': 5.802,
     'lambda_q1_2': 2.673,
     'subln_g_2': 4.763}
    for name, (base, spread) in spreads.items():
        noise = np.random.default_rng([zlib.crc32(name.encode()), seed]).standard_normal(out[name].shape)
        drawn = base * np.exp(spread * noise) if base else spread * noise
        out[name] = jnp.asarray(drawn.astype(out[name].dtype))
    for name, factor in factors.items():
        out[name] = (out[name] * factor).astype(out[name].dtype)
    return out
```

```python
import math

import numpy as np
import concourse.bass as bass
from concourse import mybir
from contextlib import ExitStack

F32 = mybir.dt.float32
F32R = mybir.dt.float32r
ACT = mybir.ActivationFunctionType
ALU = mybir.AluOpType
AX = mybir.AxisListType
ds = bass.ds

P = 128
D = 2048
KT = D // P
L = 256
T = 512
C = T // P
ROW = 64
HG = 8
TS = 8
TAPS = 5
EPS = 1e-6
BIG = 1e30
LEVELS = 7
HEADS = 8
DK = 64
BUCKETS = 32
LAYERS = 2
FQ = 4

U_ADA = 0
U_SMALL = 48
U_GDN = U_SMALL + 1
U_BC = U_GDN + 4 * HG
U_SSD = U_BC + 4
U_WOUT = U_SSD + 2 * TS
U_LAYER = U_WOUT + KT
N_IN2 = 6 * HEADS
N_LAYER = N_IN2 + KT + 2 * FQ * KT
N_UNITS = U_LAYER + LAYERS * N_LAYER
RAW = 4
SPL = 2

CONST = {"ident": 0, "ones": P, "flip": 2 * P, "blk": 3 * P, "sel": 4 * P}
KEEP = 4 * P + 8
CONST.update({"tri": KEEP, "pos": KEEP + 2 * P, "neg": KEEP + 4 * P, "level": KEEP + 6 * P})
N_CONST = KEEP + (6 + 2 * LEVELS) * P
DIST = 384

PAR, _at = {}, 0
for _name, _w in (("c", 2 * KT), ("b_ada", 48), ("pre", KT), ("post", KT), ("conv_ssd", 12 * TAPS), ("bias_ssd", 12),
                  ("conv_gdn", 24 * TAPS), ("sign", 1), ("dt_bias", 1), ("a_log", 1), ("mul", 1), ("skip", TS),
                  ("ssd_norm", TS), ("gdn_norm", 1), ("attn_norm", LAYERS * KT), ("mlp_norm", LAYERS * KT),
                  ("conv2", LAYERS * HEADS * 3), ("qg", LAYERS), ("kg", LAYERS), ("subln", LAYERS),
                  ("lam", LAYERS * 4 * DK)):
    PAR[_name] = (_at, _w)
    _at += _w
N_PAR = _at

PADW = 4 * (ROW + 2) + 2
PADT = PADW + L + 2
MLP_ORDER = (("up", 0), ("up", 1), ("down", 0), ("up", 2), ("down", 1), ("up", 3), ("down", 2), ("down", 3))
KINDS_G = ("raw", "cum", "beta", "kb", "end", "dec")
KINDS_S = ("raw", "cum", "dt", "dte", "dec")
ORDER = ((2, 3, 0, 1), (3, 2, 1, 0))


def constants():
    i, j = np.arange(P)[:, None], np.arange(P)[None, :]
    out = np.zeros((P, N_CONST), np.float32)

    def put(name, k, a):
        at = CONST[name] + k * P
        out[:, at:at + P] = a
    put("ident", 0, i == j)
    put("ones", 0, 1.0)
    put("flip", 0, i + j == P - 1)
    put("blk", 0, i // DK == j // DK)
    for r in range(4):
        out[r, CONST["sel"] + r % 2] = 1.0
    for d in range(2):
        le = i <= j if d == 0 else i >= j
        lt = j < i if d == 0 else j > i
        put("tri", d, le)
        put("pos", d, np.where(lt, 0.0, BIG))
        put("neg", d, np.where(le, 0.0, -BIG))
        for level in range(LEVELS):
            s = 1 << level
            a, b = (i, j) if d == 0 else (j, i)
            put("level", d * LEVELS + level,
                (a // (2 * s) == b // (2 * s)) & (a // s % 2 == 1) & (b // s % 2 == 0))
    return out


def bucket_rows():
    dist = 255 - np.arange(DIST)
    n = np.maximum(dist, 0)
    exact = BUCKETS // 2
    nf = np.maximum(n, exact).astype(np.float32)
    ratio = np.log(nf / np.float32(exact)) / np.float32(math.log(128 / exact))
    large = exact + (ratio * np.float32(BUCKETS - exact)).astype(np.int32)
    bucket = np.where(n < exact, n, np.minimum(large, BUCKETS - 1))
    bucket = np.where(dist < 0, BUCKETS, bucket)
    return (np.arange(BUCKETS + 1)[:, None] == bucket[None, :]).astype(np.float32)


class Unit:

    def __init__(self, c, i=0, groups=1):
        self.c, self.i, self.groups = c, i, groups
        self.n = c + i * (4 * groups)
        self.raw = c % RAW
        self.turn = c // RAW + i * groups
        self.slot = c % SPL
        self.bank = c % 2

    def ahead(self, k):
        return Unit(self.c + k, self.i, self.groups)


class Chain:

    def __init__(self, eng, sem):
        self.eng, self.sem, self.base, self.n = eng, sem, 0, 0

    def begin(self, i, per):
        self.before, self.per = self.base + self.n, per
        self.base, self.n = self.before + i * per, 0

    def end(self, turns):
        assert self.n == self.per, f"{self.n} counted instructions in a turn, not {self.per}"
        self.base, self.n = self.before + turns * self.per, 0

    def add(self, instruction):
        instruction.then_inc(self.sem, 1)
        self.n += 1

    def wait(self):
        self.eng.wait_ge(self.sem, self.base + self.n)

    def link(self, instruction):
        self.add(instruction)
        self.wait()


def build(nc, stream, x_dram, const_dram, bucket_dram, par_dram, rel_dram, out_dram, scratch, dbg=None, stop=None):
    ctx = ExitStack()
    with ctx:
        def sem(name):
            return ctx.enter_context(nc.semaphore(name))

        arena = ctx.enter_context(nc.sbuf_tensor("arena", [P, 53200], F32))
        top = {"at": 0}
        base = 0

        def put(name, cols, dt=F32, at=None):
            if at is None:
                at = top["at"]
                top["at"] = at + 4 * cols
            assert at + 4 * cols <= 4 * 53200, (name, at + 4 * cols - 4 * 53200)
            assert at % 32 == 0, (name, at)
            return nc.alloc_sbuf_tensor_at(name, [P, cols], dt, offset=ARENA0 + at)

        ARENA0 = nc.sbuf_base - 4 * 53200
        raw = [put(f"raw{r}", D) for r in range(RAW)]
        w_hi = [put(f"w_hi{s}", D, F32R) for s in range(SPL)]
        w_lo = [put(f"w_lo{s}", D, F32R) for s in range(SPL)]
        a_hi = put("a_hi", KT * T, F32R)
        a_lo = put("a_lo", KT * T, F32R)
        x_res = put("x_res", KT * L)
        relb = put("relb", 16, at=4 * (RAW * D + 2 * SPL * D + 2 * KT * T))
        onehot = put("onehot", DIST, at=4 * (RAW * D + 2 * SPL * D + 2 * KT * T + 16))
        by_dist = put("by_dist", DIST, at=4 * (RAW * D + 2 * SPL * D + 2 * KT * T + 16 + DIST))
        keep = put("keep", KEEP)
        pars = put("pars", (N_PAR + 7) // 8 * 8)
        mods = put("mods", 96)
        cols = put("cols", 8)
        shared = top["at"]
        masks = put("masks", N_CONST - KEEP)
        wk_g = put("wk_g", HG * 48)
        wk_s = put("wk_s", TS * 80)
        scans = top["at"]
        xr = put("xr", KT * T)
        xsq = put("xsq", 2 * T)
        rs1 = put("rs1", T)
        ln1 = put("ln1", T)
        mrow = put("mrow", 512)
        cs = put("cs", 2 * KT)
        c4 = put("c4", 4 * KT, F32R)
        coef = put("coef", 2 * KT)
        top["at"] = scans
        sm = put("sm", T)
        sm_e = put("sm_e", T)
        tm = put("tm", C * P)
        gcum, gtot, gend, gexp, gdec = (put(n, C * 48) for n in ("gcum", "gtot", "gend", "gexp", "gdec"))
        gmul = put("gmul", 8)
        top["at"] = scans
        g_pad = [put(f"g_pad{j}", w) for j, w in enumerate((272, 528, 528))]
        g_acc = [put(f"g_acc{j}", w) for j, w in enumerate((264, 520, 520))]
        g_A = put("g_A", 4 * P, at=top["at"] - 4 * 2 * 520)
        g_qd = put("g_qd", 4 * P, at=top["at"] - 4 * 520)
        g_q = put("g_q", L)
        g_k = put("g_k", T)
        g_v = put("g_v", T)
        g_w = put("g_w", 48)
        g_L = put("g_L", 8 * P)
        g_M = [put(f"g_M{j}", 8 * P) for j in range(2)]
        g_X = put("g_X", 8 * P)
        g_U = put("g_U", 8 * P)
        g_T = put("g_T", 8 * P)
        g_kb, g_ke, g_vb = g_X, g_M[0], g_M[1]
        g_vn = put("g_vn", 2 * P)
        g_S = put("g_S", 2 * P)
        top["at"] = scans
        s_pad = put("s_pad", 528)
        s_acc = put("s_acc", 520)
        s_bt = put("s_bt", 2 * T)
        s_ct = put("s_ct", 2 * L)
        s_btok = put("s_btok", 2 * T)
        s_cb = put("s_cb", 2 * L)
        s_x = put("s_x", T)
        s_w = put("s_w", 80)
        s_dt = put("s_dt", 2 * L)
        s_de = put("s_de", 2 * T)
        s_M = put("s_M", 8 * P)
        s_C = put("s_C", 8 * P)
        s_H = put("s_H", 6 * P)
        s_y = put("s_y", L)
        s_r = put("s_r", L)
        top["at"] = shared
        h_hi = put("h_hi", KT * L, F32R)
        turned = put("turned", KT * L, at=shared)
        h_lo = put("h_lo", KT * L, F32R)
        mo = put("mo", KT * L, at=shared + 4 * KT * L)
        bias = put("bias", 2 * HEADS * L, at=4 * (RAW * D + 2 * SPL * D + KT * L))
        n_sq, n_acc, n_ln, n_rs = (put(n, L) for n in ("n_sq", "n_acc", "n_ln", "n_rs"))
        hbuf = put("hbuf", 4 * L)
        small = put("small", 64)
        b_qk = put("b_qk", 2 * L)
        b_qs = put("b_qs", 2 * L)
        b_rs = put("b_rs", 2 * L)
        b_v = put("b_v", L)
        b_vt = put("b_vt", L)
        b_gb = put("b_gb", L)
        b_gc = put("b_gc", L)
        b_ci = put("b_ci", L)
        b_cm = put("b_cm", L + 8)
        b_co = put("b_co", L)
        b_pt = put("b_pt", 3 * P)
        b_o = put("b_o", L)
        b_s = hbuf[:, 0:768]
        b_st = put("b_st", 16)
        psum = [ctx.enter_context(nc.psum_tensor(f"bank{k}", [P, 512], F32)) for k in range(8)]

        def K(name, k=0, w=P):
            at = CONST[name] + k * P
            return keep[:, at:at + w] if at < KEEP else masks[:, at - KEEP:at - KEEP + w]

        def par(name, k=0, w=1):
            at = PAR[name][0]
            return pars[:, ds(at + k, w)] if not isinstance(k, int) else pars[:, at + k:at + k + w]

        IDENT, ONES = K("ident"), K("ones")
        EPS_C, QS_C, ONE_C, ZERO_C = (cols[:, k:k + 1] for k in range(4))

        raw_ready = [sem(f"raw_ready{r}") for r in range(RAW)]
        hi_ready, lo_ready, unit_done = sem("hi_ready"), sem("lo_ready"), sem("unit_done")
        names = """ld_par ld_x ld_masks ld_rel cols_set c_silu c_ready sq1 sq1_used ss1 rs1_ready xr_ready mrow_ready
            ada_cols mods_ready u_f32 u_hi u_ready sm_lin sm_abs sm_soft sm_e1 sm_mul sm_beta sm_turned tm_ready sm_sums
            sm_cum sm_exp wk_ready left
            pads_set pad_ready conv_done qkv_ready z_ready gw_ready g_rows g_ss sq_ready gr_ready kn_ready gram
            dpre dexp tok_used l_ready aq_ready m_ready x_mm xp_ready first_ut uu_mm ut_ready nw_mm nw_ready
            vn_mm vn_ready s_mm s_ready o_mm osq_ready oss o_rs head_done
            bc_pad bc_conv bc_ready b_turned bc_tok sx_pad sx_conv sx_ready sz_ready sw_ready s_rows s_tok s_pre s_exp
            s_de_ready s_mc_ready st_mm h_ready y_mm tile_done grp_sq grp_ss grp_rs grp_done
            y_hi y_ready mo_ready acc_ready turned_ready flip_mm flip_read rel_mm rel_copy rel_out x_loaded
            ss_mm rs_ready post_ready xn_ready h_f32 h_hi_ready h_ready2
            lam_e lam_d lam_ready qk_sq ln_qk rs_qk qk_ready qk_ss score_mm v_ready vt_mm vt_ready gates_ready ci_ready
            sc_ready p_exp p_ready pt_mm pt_ready av_mm av_sq av_ss av_rs attn_f32 attn_hi conv_f32 conv_hi yt_ready
            sx_upd relu_ready sq_relu hi_relu mlp_ready x_final out_done rel_set y_set bias_ready dve_own act_own pool_own dbg_ready dbg_done""".split()
        S = {n: sem(n) for n in names}

        def split_act(act, u):
            act.wait_ge(raw_ready[u.raw], (u.turn + 1) * 16)
            if u.c >= SPL:
                act.wait_ge(unit_done, u.n - SPL + 1)
            act.copy(w_hi[u.slot][:], raw[u.raw][:]).then_inc(hi_ready, 1)

        def split_dve(dve, u):
            dve.wait_ge(hi_ready, u.n + 1)
            dve.tensor_tensor(w_lo[u.slot][:], raw[u.raw][:], w_hi[u.slot][:], ALU.subtract).then_inc(lo_ready, 1)

        def unit_mm(pe, u, hi, lo, n, bank=None):
            pe.wait_ge(lo_ready, u.n + 1)
            acc = psum[u.bank][:, 0:n]
            for k in range(KT):
                wh, wl = (w[u.slot][:, k * P:(k + 1) * P] for w in (w_hi, w_lo))
                pe.matmul(acc, wh, lo[:, k, 0:n], start=(k == 0), stop=False)
                pe.matmul(acc, wl, hi[:, k, 0:n], start=False, stop=False)
                last = pe.matmul(acc, wh, hi[:, k, 0:n], start=False, stop=(k == KT - 1))
            last.then_inc(unit_done, 1)

        u_hi3, u_lo3 = (a[:].rearrange("p (k t) -> p k t", t=T) for a in (a_hi, a_lo))
        y_hi3, y_lo3 = (a[:, 0:KT * L].rearrange("p (k t) -> p k t", t=L) for a in (a_hi, a_lo))
        h_hi3, h_lo3 = (a[:].rearrange("p (k t) -> p k t", t=L) for a in (h_hi, h_lo))

        def leave(eng, k):
            eng.drain().then_inc(S["left"], 1)
            eng.wait_ge(S["left"], 4 * k)

        def d3(ap, n):
            return ap.rearrange("p (a b) -> p a b", b=n)

        def rows4(ap):
            return ap.rearrange("p (r w) -> p r w", w=ROW + 2)[:, :, 0:ROW]

        def bc(ap2, n):
            return ap2.unsqueeze(2).broadcast_to([P, ap2.shape[1], n])

        def over(ap2, n):
            return ap2.unsqueeze(1).broadcast_to([P, n, ap2.shape[1]])

        block = ctx.enter_context(nc.Block())

        @block.sync
        def _(sp):
            def load(n, r, wait):
                if wait is not None:
                    sp.wait_ge(lo_ready, wait)
                sp.dma_start(raw[r][:], stream[ds(n, 1) if not isinstance(n, int) else slice(n, n + 1)]
                             .rearrange("a p m -> p (a m)")).then_inc(raw_ready[r], 16)

            for n in range(RAW):
                load(n, n, None)
            with sp.Fori(1, N_UNITS // RAW) as i:
                for r in range(RAW):
                    load(i * RAW + r, r, i * RAW + (r - RAW + 1))
            for n in range(N_UNITS // RAW * RAW, N_UNITS):
                load(n, n % RAW, n - RAW + 1)
            for q in range(4):
                sp.wait_ge(S["x_final"], 4 * (q + 1))
                sp.dma_start(out_dram[q * 512:(q + 1) * 512, :].rearrange("(k p) t -> p k t", p=P),
                             d3(x_res[:, q * 4 * L:(q + 1) * 4 * L], L)).then_inc(S["out_done"], 16)
            sp.wait_ge(S["out_done"], 64)
            sp.wait_ge(S["rel_out"], 32)

        @block.gpsimd
        def _(pool):
            own = Chain(pool, S["pool_own"])
            pool.dma_start(relb[0:BUCKETS, :], rel_dram).then_inc(S["ld_rel"], 16)
            pool.dma_start(onehot[0:BUCKETS + 1, :], bucket_dram).then_inc(S["ld_rel"], 16)
            pool.memset(relb[BUCKETS:BUCKETS + 1, :], -BIG).then_inc(S["rel_set"], 1)
            pool.dma_start(masks[:], const_dram[:, KEEP:N_CONST]).then_inc(S["ld_masks"], 16)
            pool.wait_ge(S["rel_set"], 1)
            pool.memset(EPS_C, EPS)
            pool.memset(QS_C, -0.5 * math.log(HG * 16))
            pool.memset(ONE_C, 1.0)
            pool.memset(ZERO_C, 0.0).then_inc(S["cols_set"], 1)
            leave(pool, 1)
            leave(pool, 2)
            for j in range(3):
                last = pool.memset(g_pad[j][:], 0.0)
            last.then_inc(S["pads_set"], 1)

            with pool.Fori(0, HG) as i:
                pool.wait_ge(S["head_done"], i + 1)
                pool.tensor_copy(g_w[:], wk_g[:, ds(i * 48, 48)]).then_inc(S["gw_ready"], 1)
                pool.wait_ge(S["l_ready"], i + 1)
                for level in range(LEVELS):
                    if level >= 2:
                        pool.wait_ge(S["x_mm"], i * (2 * LEVELS) + 2 * (level - 1))
                    if level == 2:
                        pool.wait_ge(S["first_ut"], i + 1)
                    for d in range(2):
                        m = pool.tensor_tensor(d3(g_M[level % 2][:, d * 512:d * 512 + 512], P),
                                               d3(g_L[:, d * 512:d * 512 + 512], P),
                                               over(K("level", d * LEVELS + level), 4), ALU.mult)
                    m.then_inc(S["m_ready"], 1)

            leave(pool, 3)
            pool.memset(s_pad[:], 0.0).then_inc(S["pads_set"], 1)
            for g in range(2):
                with pool.Fori(0, 2) as i:
                    for a in range(2):
                        pool.wait_ge(S["tile_done"], i * 2 + (4 * g + a + 1))
                        pool.tensor_copy(s_w[:], wk_s[:, ds(i * 160 + (g * 4 + a) * 80, 80)]).then_inc(S["sw_ready"], 1)
            leave(pool, 4)
            pool.wait_ge(S["rel_out"], 16)
            pool.dma_start(d3(turned[:], L), bass.AP(scratch[0].tensor, 0, [[1, P], [DIST, 2 * HEADS], [1, L]])
                           ).then_inc(S["turned_ready"], 16)
            for e in range(1 + 2 * LAYERS):
                if e:
                    pool.wait_ge(S["ss_mm"], e)
                own.add(pool.memset(n_acc[:], 0.0))
                src, ready, at = (mo, S["mo_ready"], 0) if e == 0 else (x_res, S["sx_upd"], (e - 1) * KT)
                with pool.Fori(0, KT) as i:
                    own.begin(i, 2)
                    pool.wait_ge(ready, i + (at + 1))
                    tile = src[:, ds(i * L, L)]
                    own.link(pool.tensor_tensor(n_sq[:], tile, tile, ALU.mult))
                    own.link(pool.tensor_tensor(n_acc[:], n_acc[:], n_sq[:], ALU.add))
                own.end(KT)
                pool.tensor_copy(n_sq[:], n_acc[:]).then_inc(S["acc_ready"], 1)
                if e and e % 2 == 0:
                    l = e // 2 - 1
                    for q in range(FQ):
                        with pool.Fori(0, KT // 4) as i:
                            for j in range(4):
                                at = l * FQ * KT + q * KT + j + 1
                                pool.wait_ge(S["relu_ready"], i * 4 + at)
                                pool.wait_ge(S["mlp_ready"], i * 4 + at)
                                t = hbuf[:, (j % 2) * L:(j % 2) * L + L]
                                s = hbuf[:, (2 + j % 2) * L:(3 + j % 2) * L]
                                pool.tensor_tensor(s, t, t, ALU.mult).then_inc(S["sq_relu"], 1)

        @block.tensor
        def _(pe):
            mm = pe.matmul

            def each(bank, pairs, w=P, at=0):
                for n, (lhs, rhs) in enumerate(pairs):
                    last = mm(psum[bank][:, at + n * w:at + (n + 1) * w], lhs, rhs, start=True, stop=True)
                return last

            def turn(bank, tiles, at=0):
                for n, t in enumerate(tiles):
                    last = pe.transpose(psum[bank][:, at + n * P:at + (n + 1) * P], t, IDENT)
                return last

            def blocks(buf, d, n=4):
                return [buf[:, (d * n + c) * P:(d * n + c + 1) * P] for c in range(n)]

            pe.wait_ge(S["ld_par"], 32)
            pe.wait_ge(S["ld_rel"], 32)
            pe.wait_ge(S["rel_set"], 1)
            mm(psum[5][0:16, 0:DIST], relb[0:BUCKETS + 1, :], onehot[0:BUCKETS + 1, :], start=True, stop=True).then_inc(S["rel_mm"], 1)

            for k in range(KT):
                pe.wait_ge(S["sq1"], k + 1)
                m = mm(psum[4][:], ONES, xsq[:, (k % 2) * T:(k % 2) * T + T], start=(k == 0), stop=(k == KT - 1))
                m.then_inc(S["sq1_used"], 1)

            pe.wait_ge(S["c_ready"], 1)
            with pe.Fori(0, 12) as i:
                for q in range(4):
                    u = Unit(q, i)
                    pe.wait_ge(lo_ready, u.n + 1)
                    for k in range(4):
                        cw = c4[:, (q * 4 + k) * 4:(q * 4 + k) * 4 + 4]
                        mm(psum[2][0:4, :], cw, w_hi[u.slot][:, k * 512:(k + 1) * 512], start=(q + k == 0), stop=False)
                        m = mm(psum[2][0:4, :], cw, w_lo[u.slot][:, k * 512:(k + 1) * 512], start=False, stop=(q * 4 + k == 15))
                    m.then_inc(unit_done, 1)
                pe.wait_ge(S["mrow_ready"], i + 1)
                for j in range(4):
                    m = mm(psum[3][:, ds(i * 8 + j * 2, 2)], mrow[0:4, j * P:(j + 1) * P], K("sel", 0, 2)[0:4, :],
                           start=True, stop=True)
                m.then_inc(S["ada_cols"], 1)

            pe.wait_ge(S["u_ready"], KT)
            unit_mm(pe, Unit(U_SMALL), u_hi3, u_lo3, T)
            leave(pe, 1)
            pe.wait_ge(S["sm_beta"], 1)
            turn(2, [sm_e[:, c * P:(c + 1) * P] for c in range(C)]).then_inc(S["sm_turned"], 1)
            pe.wait_ge(S["tm_ready"], 1)
            pe.wait_ge(S["ld_masks"], 16)
            log = d3(tm[:], P)[:, :, 0:48]
            for d in range(2):
                mm(d3(psum[3][:, d * 192:d * 192 + 192], 48), K("tri", d), log, start=True, stop=True)
            mm(d3(psum[4][:, 0:192], 48), ONES, log, start=True, stop=True).then_inc(S["sm_sums"], 1)
            leave(pe, 2)

            with pe.Fori(0, HG) as i:
                unit_mm(pe, Unit(U_GDN, i), u_hi3, u_lo3, L)
                unit_mm(pe, Unit(U_GDN + 1, i), u_hi3, u_lo3, T)
                unit_mm(pe, Unit(U_GDN + 2, i), u_hi3, u_lo3, T)
                pe.wait_ge(S["head_done"], i + 1)
                pe.wait_ge(S["gw_ready"], i + 1)
                for d in range(2):
                    m = each(6 + d, [(g_w[:, d * 4 + c:d * 4 + c + 1].broadcast_to([P, P]), K("tri", d)) for c in range(C)])
                m.then_inc(S["g_rows"], 1)
                unit_mm(pe, Unit(U_GDN + 3, i), u_hi3, u_lo3, L)
                pe.wait_ge(S["sq_ready"], i + 1)
                mm(psum[2][:], ONES, g_X[:, 0:T], start=True, stop=True)
                mm(psum[3][:, 0:L], ONES, g_X[:, T:T + L], start=True, stop=True).then_inc(S["g_ss"], 1)
                pe.wait_ge(S["kn_ready"], i + 1)
                kn = [g_k[:, c * P:(c + 1) * P] for c in range(C)]
                each(4, [(k, k) for k in kn]).then_inc(S["gram"], 1)
                each(5, [(kn[c], g_q[:, c * P:(c + 1) * P]) for c in range(2)]).then_inc(S["gram"], 1)
                pe.wait_ge(S["m_ready"], i * LEVELS + 1)
                for d in range(2):
                    m = turn(2 + d, blocks(g_M[0], d))
                    m.then_inc(S["x_mm"], 1)
                for level in range(1, LEVELS):
                    pe.wait_ge(S["m_ready"], i * LEVELS + (level + 1))
                    for d in range(2):
                        if level == 1:
                            pe.wait_ge(S["first_ut"], i + 1)
                        else:
                            pe.wait_ge(S["ut_ready"], i * 12 + (2 * (level - 2) + d + 1))
                        each(4 + d, zip(blocks(g_M[level % 2], d), blocks(g_U, d))).then_inc(S["x_mm"], 1)
                    for d in range(2):
                        pe.wait_ge(S["xp_ready"], i * 12 + (2 * (level - 1) + d + 1))
                        m = each(6 + d, zip(blocks(g_T, d), blocks(g_X, d)))
                        if level < LEVELS - 1:
                            m = each(2 + d, zip(blocks(g_X, d), blocks(g_T, d)))
                        m.then_inc(S["uu_mm"], 1)
                turn(2, kn).then_inc(S["nw_mm"], 1)
                turn(3, [g_v[:, c * P:(c + 1) * P] for c in range(C)]).then_inc(S["nw_mm"], 1)
                pe.wait_ge(S["tok_used"], i * 2 + 1)
                for d in range(2):
                    pe.wait_ge(S["ut_ready"], i * 12 + (10 + d + 1))
                    each(4 + d, zip(blocks(g_kb, d), blocks(g_U, d))).then_inc(S["nw_mm"], 1)
                pe.wait_ge(S["aq_ready"], i + 1)
                pe.wait_ge(S["tok_used"], i * 2 + 2)
                for step in range(4):
                    for d in range(2):
                        c = ORDER[d][step]
                        b = d * 4 + c
                        if step == 0:
                            pe.wait_ge(S["nw_ready"], i * 2 + (d + 1))
                        else:
                            pe.wait_ge(S["s_ready"], i * 6 + (2 * (step - 1) + d + 1))
                        vn = psum[6 + d][:, 0:P]
                        m = mm(vn, g_U[:, b * P:(b + 1) * P], g_vb[:, b * P:(b + 1) * P], start=True, stop=(step == 0))
                        if step:
                            m = mm(vn, g_T[:, b * P:(b + 1) * P], g_S[:, d * P:(d + 1) * P], start=False, stop=True)
                        m.then_inc(S["vn_mm"], 1)
                        if step >= 2:
                            a = d * 2 + c
                            mm(psum[4][:, c * P:(c + 1) * P], g_S[:, d * P:(d + 1) * P], g_qd[:, a * P:(a + 1) * P],
                               start=(step == 2 and d == 0), stop=False, skip_group_check=True)
                    for d in range(2):
                        c = ORDER[d][step]
                        b = d * 4 + c
                        pe.wait_ge(S["vn_ready"], i * 8 + (2 * step + d + 1))
                        v = g_vn[:, d * P:(d + 1) * P]
                        if step < 3:
                            mm(psum[2 + d][:, 0:P], g_ke[:, b * P:(b + 1) * P], v, start=True, stop=True).then_inc(S["s_mm"], 1)
                        if step >= 2:
                            a = d * 2 + c
                            m = mm(psum[4][:, c * P:(c + 1) * P], v, g_A[:, a * P:(a + 1) * P],
                                   start=False, stop=(step == 3), skip_group_check=True)
                m.then_inc(S["o_mm"], 1)
                pe.wait_ge(S["osq_ready"], i + 1)
                mm(psum[5][:, 0:L], ONES, g_X[:, 0:L], start=True, stop=True).then_inc(S["oss"], 1)

            leave(pe, 3)
            for j in range(4):
                unit_mm(pe, Unit(U_BC + j), u_hi3, u_lo3, T if j < 2 else L)
            pe.wait_ge(S["bc_ready"], 4)
            for g in range(2):
                m = turn(2 + g, [s_bt[:, g * T + c * P:g * T + (c + 1) * P] for c in range(C)])
            for g in range(2):
                m = each(4, [(s_bt[:, g * T + c * P:g * T + (c + 1) * P], s_ct[:, g * L + c * P:g * L + (c + 1) * P])
                             for c in range(2)], at=g * 2 * P)
            m.then_inc(S["b_turned"], 1)
            for g in range(2):
                with pe.Fori(0, 2) as i:
                    for a in range(2):
                        t = g * 4 + a
                        unit_mm(pe, Unit(U_SSD + 2 * t, i), u_hi3, u_lo3, T)
                        pe.wait_ge(S["tile_done"], i * 2 + (t + 1))
                        pe.wait_ge(S["sw_ready"], i * 2 + (t + 1))
                        pe.wait_ge(S["bc_tok"], 1)
                        for d in range(2):
                            m = each(3 + d, [(s_w[:, d * 8 + e:d * 8 + e + 1].broadcast_to([P, P]), K("tri", d))
                                             for e in range(4)])
                        m.then_inc(S["s_rows"], 1)
                        unit_mm(pe, Unit(U_SSD + 2 * t + 1, i), u_hi3, u_lo3, L)
                        pe.wait_ge(S["sx_ready"], i * 2 + (t + 1))
                        turn(2, [s_x[:, c * P:(c + 1) * P] for c in range(C)]).then_inc(S["s_tok"], 1)
                        pe.wait_ge(S["s_de_ready"], i * 2 + (t + 1))
                        for d in range(2):
                            m = each(5 + d, [(s_btok[:, g * T + c * P:g * T + (c + 1) * P],
                                              s_de[:, (d * 4 + c) * P:(d * 4 + c + 1) * P]) for c in ORDER[d][0:3]])
                        m.then_inc(S["st_mm"], 1)
                        pe.wait_ge(S["s_mc_ready"], i * 2 + (t + 1))
                        pe.wait_ge(S["h_ready"], i * 2 + (t + 1))
                        for e in range(2):
                            for c in range(2):
                                o = psum[7][e * 64:e * 64 + 64, c * P:(c + 1) * P]
                                for d in range(2):
                                    b = (d * 2 + c) * 2 + e
                                    x = s_dt[:, (d * 2 + c) * P + e * 64:(d * 2 + c) * P + e * 64 + 64]
                                    mm(o, x, s_M[:, b * P:(b + 1) * P], start=(c == 0 and d == 0), stop=False, skip_group_check=True)
                                    s = (d * 3 + ORDER[d].index(c) - 1) * P + e * 64
                                    m = mm(o, s_H[:, s:s + 64], s_C[:, b * P:(b + 1) * P], start=False, stop=(d == 1),
                                           skip_group_check=True)
                        m.then_inc(S["y_mm"], 1)
                pe.wait_ge(S["grp_sq"], g + 1)
                for k in range(4):
                    m = mm(psum[2][:, 0:L], ONES, s_M[:, k * L:(k + 1) * L], start=(k == 0), stop=(k == 3))
                m.then_inc(S["grp_ss"], 1)
            leave(pe, 4)

            pe.wait_ge(S["y_ready"], 4)
            with pe.Fori(0, KT // 4) as i:
                for j in range(4):
                    unit_mm(pe, Unit(U_WOUT + j, i), y_hi3, y_lo3, L)

            def norm_sums(e):
                pe.wait_ge(S["acc_ready"], e + 1)
                mm(psum[2][:, 0:L], ONES, n_sq[:], start=True, stop=True).then_inc(S["ss_mm"], 1)

            norm_sums(0)
            pe.wait_ge(S["turned_ready"], 16)
            for k in range(8):
                if k >= 2:
                    pe.wait_ge(S["flip_read"], k - 1)
                mm(psum[6 + k % 2][:], K("flip"), turned[:, k * 512:(k + 1) * 512], start=True, stop=True).then_inc(S["flip_mm"], 1)
            for l in range(LAYERS):
                base = U_LAYER + l * N_LAYER
                norm_sums(1 + 2 * l)
                pe.wait_ge(S["h_ready2"], (2 * l + 1) * 8)
                with pe.Fori(0, HEADS // 2) as i:
                    for j in range(2):
                        def at(n, k):
                            return i * (2 * n) + ((l * HEADS + j) * n + k)
                        u = Unit(base + 6 * j, i, 3)
                        unit_mm(pe, u, h_hi3, h_lo3, L)
                        unit_mm(pe, u.ahead(1), h_hi3, h_lo3, L)
                        unit_mm(pe, u.ahead(2), h_hi3, h_lo3, L)
                        pe.wait_ge(S["qk_sq"], at(2, 2))
                        mm(psum[2][:], K("blk"), b_qs[:], start=True, stop=True).then_inc(S["qk_ss"], 1)
                        unit_mm(pe, u.ahead(3), h_hi3, h_lo3, L)
                        pe.wait_ge(S["qk_ready"], at(1, 1))
                        for m_ in range(2):
                            rows = slice(m_ * DK, (m_ + 1) * DK)
                            mm(psum[3 + m_][:, 0:L], b_qk[rows, P:L], b_qk[rows, L:2 * L], start=True, stop=True)
                            m = mm(psum[3 + m_][:, L:L + P], b_qk[rows, 0:P], b_qk[rows, L:L + P], start=True, stop=True)
                        m.then_inc(S["score_mm"], 1)
                        pe.wait_ge(S["v_ready"], at(1, 1))
                        turn(5, [b_v[:, 0:P], b_v[:, P:L]]).then_inc(S["vt_mm"], 1)
                        unit_mm(pe, u.ahead(4), h_hi3, h_lo3, L)
                        unit_mm(pe, u.ahead(5), h_hi3, h_lo3, L)
                        pe.wait_ge(S["p_ready"], at(1, 1))
                        turn(6, [b_s[:, L:L + P], b_s[:, 0:P], b_s[:, P:L]]).then_inc(S["pt_mm"], 1)
                        pe.wait_ge(S["pt_ready"], at(1, 1))
                        pe.wait_ge(S["vt_ready"], at(1, 1))
                        mm(psum[7][:, 0:L], b_vt[:, 0:P], b_pt[:, 0:L], start=True, stop=False, skip_group_check=True)
                        mm(psum[7][:, P:L], b_vt[:, P:L], b_pt[:, L:L + P], start=False, stop=True,
                           skip_group_check=True).then_inc(S["av_mm"], 1)
                        pe.wait_ge(S["av_sq"], at(1, 1))
                        mm(psum[2][:, 0:L], ONES, b_qs[:, 0:L], start=True, stop=True).then_inc(S["av_ss"], 1)
                pe.wait_ge(S["yt_ready"], (l + 1) * 2 * HEADS)
                with pe.Fori(0, KT // 4) as i:
                    for j in range(4):
                        unit_mm(pe, Unit(base + N_IN2 + j, i), y_hi3, y_lo3, L)
                norm_sums(2 + 2 * l)
                pe.wait_ge(S["h_ready2"], (2 * l + 2) * 8)
                c = base + N_IN2 + KT
                for kind, q in MLP_ORDER:
                    if kind == "up":
                        hi, lo = h_hi3, h_lo3
                    else:
                        pe.wait_ge(S["mlp_ready"], (l * FQ + q + 1) * KT + 2)
                        hi, lo = (a[:, (q % 2) * KT * L:(q % 2 + 1) * KT * L].rearrange("p (k t) -> p k t", t=L)
                                  for a in (a_hi, a_lo))
                    with pe.Fori(0, KT // 4) as i:
                        for j in range(4):
                            unit_mm(pe, Unit(c + j, i), hi, lo, L)
                    c += KT

        @block.scalar
        def _(act):
            own = Chain(act, S["act_own"])
            f = act.activation

            def root(out, in_, tmp, scale, last, bias=None):
                own.link(f(tmp, in_, ACT.Ln, bias=EPS_C, scale=scale))
                f(out, tmp, ACT.Exp, bias=ZERO_C if bias is None else bias, scale=-0.5).then_inc(S[last], 1)

            act.dma_start(keep[:], const_dram[:, 0:KEEP]).then_inc(S["ld_par"], 16)
            act.dma_start(pars[:, 0:N_PAR], par_dram).then_inc(S["ld_par"], 16)
            act.dma_start(d3(xr[:], T), x_dram.rearrange("(k p) t -> p k t", p=P)).then_inc(S["ld_x"], 16)
            act.wait_ge(S["ld_par"], 32)
            act.wait_ge(S["cols_set"], 1)
            own.link(f(cs[:], par("c", 0, 2 * KT), ACT.Silu))
            act.copy(d3(c4[:], 4)[:, :, 0:2], d3(cs[:], 2)).then_inc(S["c_silu"], 1)
            act.wait_ge(S["ld_x"], 16)
            for k in range(KT):
                if k >= 2:
                    act.wait_ge(S["sq1_used"], k - 1)
                f(xsq[:, (k % 2) * T:(k % 2) * T + T], xr[:, k * T:(k + 1) * T], ACT.Square).then_inc(S["sq1"], 1)
            split_act(act, Unit(0))
            split_act(act, Unit(1))
            act.wait_ge(S["sq1_used"], KT)
            root(rs1[:], psum[4][:], ln1[:], 1.0 / D, "rs1_ready")
            act.wait_ge(S["rel_copy"], 1)
            act.dma_start(scratch[0], by_dist[0:16, :]).then_inc(S["rel_out"], 16)
            with act.Fori(0, 12) as i:
                for q in range(4):
                    u = Unit(q, i)
                    act.wait_ge(unit_done, u.n + 1)
                    if q == 3:
                        act.copy(mrow[0:4, :], psum[2][0:4, :]).then_inc(S["mrow_ready"], 1)
                    split_act(act, u.ahead(2))
            for k in range(KT):
                act.wait_ge(S["u_f32"], k + 1)
                act.copy(a_hi[:, k * T:(k + 1) * T], xr[:, k * T:(k + 1) * T]).then_inc(S["u_hi"], 1)
            leave(act, 1)
            act.wait_ge(S["sm_lin"], 1)
            own.link(f(sm_e[:], sm[:], ACT.Abs))
            own.link(f(sm_e[:], sm_e[:], ACT.Exp, scale=-1.0))
            f(gmul[:, 0:1], par("a_log"), ACT.Exp)
            f(sm_e[:], sm_e[:], ACT.Ln, bias=ONE_C).then_inc(S["sm_soft"], 1)
            split_act(act, Unit(U_SMALL + 2))
            act.wait_ge(S["sm_mul"], 1)
            f(sm_e[64:96, :], sm[64:96, :], ACT.Exp, scale=-1.0).then_inc(S["sm_beta"], 1)
            act.wait_ge(S["sm_turned"], 1)
            act.copy(tm[:], psum[2][:]).then_inc(S["tm_ready"], 1)
            act.wait_ge(S["sm_cum"], 1)
            f(gexp[:], gcum[:], ACT.Exp)
            f(gdec[:], gtot[:], ACT.Exp)
            f(gend[:], gend[:], ACT.Exp).then_inc(S["sm_exp"], 1)
            leave(act, 2)

            act.wait_ge(S["pads_set"], 1)
            act.wait_ge(S["rel_out"], 16)
            with act.Fori(0, HG) as i:
                own.begin(i, 4)
                u = Unit(U_GDN, i)

                def padded(j):
                    v = u.ahead(j)
                    act.wait_ge(unit_done, v.n + 1)
                    bank = psum[v.bank]
                    m = act.copy(rows4(g_pad[j][:, 2:PADW]), d3(bank[:, 0:L], ROW))
                    if j:
                        m = act.copy(g_pad[j][:, PADW:PADW + L], bank[:, L:T])
                    m.then_inc(S["pad_ready"], 1)
                    split_act(act, v.ahead(2))

                def silu(j, out):
                    act.wait_ge(S["conv_done"], i * 3 + (j + 1))
                    m = f(d3(out[:, 0:L], ROW), rows4(g_acc[j][:, 0:264]), ACT.Silu)
                    if j:
                        m = f(out[:, L:T], g_acc[j][:, 264:520], ACT.Silu)
                    return m
                padded(0)
                padded(1)
                act.wait_ge(S["head_done"], i + 1)
                silu(0, g_q)
                padded(2)
                own.link(silu(1, g_k))
                silu(2, g_v).then_inc(S["qkv_ready"], 1)
                z = u.ahead(3)
                act.wait_ge(unit_done, z.n + 1)
                f(x_res[:, ds(i * L + HG * L, L)], psum[z.bank][:, 0:L], ACT.Silu)
                split_act(act, z.ahead(2))
                f(g_X[:, 0:T], g_k[:], ACT.Square)
                f(g_X[:, T:T + L], g_q[:], ACT.Square).then_inc(S["sq_ready"], 1)
                act.wait_ge(S["g_ss"], i + 1)
                own.add(f(g_M[0][:, T:T + L], psum[3][:, 0:L], ACT.Ln, bias=EPS_C))
                own.link(f(g_M[0][:, 0:T], psum[2][:], ACT.Ln, bias=EPS_C))
                f(g_M[0][:, T:T + L], g_M[0][:, T:T + L], ACT.Exp, bias=QS_C, scale=-0.5)
                f(g_M[0][:, 0:T], g_M[0][:, 0:T], ACT.Exp, scale=-0.5).then_inc(S["gr_ready"], 1)
                act.wait_ge(S["dpre"], i + 1)
                f(g_L[:], g_L[:], ACT.Exp, scale=-1.0)
                f(g_A[:], g_A[:], ACT.Exp)
                f(g_qd[:, 0:L], psum[6][:, 0:L], ACT.Exp)
                f(g_qd[:, L:2 * L], psum[7][:, 0:L], ACT.Exp).then_inc(S["dexp"], 1)
                for level in range(1, LEVELS):
                    for d in range(2):
                        act.wait_ge(S["uu_mm"], i * 12 + (2 * (level - 1) + d + 1))
                        half = slice(d * 512, d * 512 + 512)
                        m = act.copy(g_U[:, half], psum[6 + d][:])
                        if level < LEVELS - 1:
                            m = act.copy(g_T[:, half], psum[2 + d][:])
                        m.then_inc(S["ut_ready"], 1)
                for d in range(2):
                    act.wait_ge(S["nw_mm"], i * 4 + (3 + d))
                    act.mul(g_T[:, d * 512:d * 512 + 512], psum[4 + d][:], -1.0).then_inc(S["nw_ready"], 1)
                for step in range(4):
                    for d in range(2):
                        act.wait_ge(S["vn_mm"], i * 8 + (2 * step + d + 1))
                        act.copy(g_vn[:, d * P:(d + 1) * P], psum[6 + d][:, 0:P]).then_inc(S["vn_ready"], 1)
                act.wait_ge(S["o_mm"], i + 1)
                f(g_X[:, 0:L], psum[4][:, 0:L], ACT.Square).then_inc(S["osq_ready"], 1)
                act.wait_ge(S["oss"], i + 1)
                root(g_M[0][:, L:2 * L], psum[5][:, 0:L], g_M[0][:, 0:L], 1.0 / P, "o_rs")
            own.end(HG)

            leave(act, 3)
            act.wait_ge(S["pads_set"], 2)
            for j in range(4):
                u = Unit(U_BC + j)
                act.wait_ge(unit_done, u.n + 1)
                bank = psum[u.bank]
                m = act.copy(rows4(s_pad[:, 2:PADW]), d3(bank[:, 0:L], ROW))
                if j < 2:
                    m = act.copy(s_pad[:, PADW:PADW + L], bank[:, L:T])
                m.then_inc(S["bc_pad"], 1)
                split_act(act, u.ahead(2))
                act.wait_ge(S["bc_conv"], j + 1)
                out = s_bt[:, j * T:(j + 1) * T] if j < 2 else s_ct[:, (j - 2) * L:(j - 1) * L]
                m = f(d3(out[:, 0:L], ROW), rows4(s_acc[:, 0:264]), ACT.Silu, bias=par("bias_ssd", 8 + j))
                if j < 2:
                    m = f(out[:, L:T], s_acc[:, 264:520], ACT.Silu, bias=par("bias_ssd", 8 + j))
                m.then_inc(S["bc_ready"], 1)
            act.wait_ge(S["b_turned"], 1)
            act.copy(s_btok[:, 0:T], psum[2][:])
            act.copy(s_btok[:, T:2 * T], psum[3][:])
            act.copy(s_cb[:], psum[4][:]).then_inc(S["bc_tok"], 1)
            for g in range(2):
                with act.Fori(0, 2) as i:
                    for a in range(2):
                        t = g * 4 + a
                        u = Unit(U_SSD + 2 * t, i)
                        act.wait_ge(unit_done, u.n + 1)
                        bank = psum[u.bank]
                        act.copy(rows4(s_pad[:, 2:PADW]), d3(bank[:, 0:L], ROW))
                        act.copy(s_pad[:, PADW:PADW + L], bank[:, L:T]).then_inc(S["sx_pad"], 1)
                        split_act(act, u.ahead(2))
                        act.wait_ge(S["tile_done"], i * 2 + (t + 1))
                        act.wait_ge(S["sx_conv"], i * 2 + (t + 1))
                        b = par("bias_ssd", i * 2 + t)
                        f(d3(s_x[:, 0:L], ROW), rows4(s_acc[:, 0:264]), ACT.Silu, bias=b)
                        f(s_x[:, L:T], s_acc[:, 264:520], ACT.Silu, bias=b).then_inc(S["sx_ready"], 1)
                        u = u.ahead(1)
                        act.wait_ge(unit_done, u.n + 1)
                        f(x_res[:, ds(i * (2 * L) + t * L, L)], psum[u.bank][:, 0:L], ACT.Silu)
                        split_act(act, u.ahead(2))
                        act.wait_ge(S["s_pre"], i * 2 + (t + 1))
                        f(s_M[:], s_M[:], ACT.Exp)
                        f(s_C[:, 0:T], psum[3][:], ACT.Exp)
                        f(s_C[:, T:2 * T], psum[4][:], ACT.Exp).then_inc(S["s_exp"], 1)
                act.wait_ge(S["tile_done"], 4 * (g + 1) + 1)
                f(s_M[:], x_res[:, g * 4 * L:(g + 1) * 4 * L], ACT.Square).then_inc(S["grp_sq"], 1)
                act.wait_ge(S["grp_ss"], g + 1)
                root(s_y[:], psum[2][:, 0:L], s_r[:], 1.0 / 512, "grp_rs")
            leave(act, 4)

            for q in range(4):
                act.copy(a_hi[:, q * 1024:(q + 1) * 1024], x_res[:, q * 1024:(q + 1) * 1024]).then_inc(S["y_hi"], 1)
            act.wait_ge(S["y_ready"], 4)
            act.dma_start(d3(x_res[:], L), x_dram[:, 0:L].rearrange("(k p) t -> p k t", p=P)).then_inc(S["x_loaded"], 16)
            with act.Fori(0, KT // 4) as i:
                for j in range(4):
                    u = Unit(U_WOUT + j, i)
                    act.wait_ge(unit_done, u.n + 1)
                    act.copy(mo[:, ds(i * (4 * L) + j * L, L)], psum[u.bank][:, 0:L]).then_inc(S["mo_ready"], 1)
                    split_act(act, u.ahead(2))

            def norm_root(e):
                act.wait_ge(S["ss_mm"], e + 1)
                root(n_rs[:], psum[2][:, 0:L], n_ln[:], 1.0 / D, "rs_ready")

            def norm_hi(e):
                for g in range(8):
                    act.wait_ge(S["h_f32"], e * 8 + g + 1)
                    act.copy(h_hi[:, g * T:(g + 1) * T], hbuf[:, (g % 2) * T:(g % 2) * T + T]).then_inc(S["h_hi_ready"], 1)

            norm_root(0)
            act.wait_ge(S["lam_d"], 1)
            f(small[:, 20:24], small[:, 16:20], ACT.Exp).then_inc(S["lam_e"], 1)
            for k in range(8):
                act.wait_ge(S["flip_mm"], k + 1)
                act.copy(bias[:, k * 512:(k + 1) * 512], psum[6 + k % 2][:]).then_inc(S["flip_read"], 1)
            act.wait_ge(S["flip_read"], 8)
            act.dma_start(scratch[1], bias[:]).then_inc(S["rel_out"], 16)
            for l in range(LAYERS):
                base = U_LAYER + l * N_LAYER
                norm_root(1 + 2 * l)
                norm_hi(2 * l)
                if l:
                    act.dma_start(bias[:], scratch[1]).then_inc(S["bias_ready"], 16)
                with act.Fori(0, HEADS // 2) as i:
                    own.begin(i, 4)
                    for j in range(2):
                        def at(n, k):
                            return i * (2 * n) + ((l * HEADS + j) * n + k)
                        u = Unit(base + 6 * j, i, 3)

                        def projected(m):
                            act.wait_ge(unit_done, u.ahead(m).n + 1)
                            return psum[u.ahead(m).bank][:, 0:L]
                        for m in range(2):
                            act.copy(b_qk[:, m * L:(m + 1) * L], projected(m))
                            f(b_qs[:, m * L:(m + 1) * L], psum[u.ahead(m).bank][:, 0:L], ACT.Square).then_inc(S["qk_sq"], 1)
                            split_act(act, u.ahead(m + 2))
                        act.copy(b_v[:], projected(2)).then_inc(S["v_ready"], 1)
                        split_act(act, u.ahead(4))
                        act.wait_ge(S["qk_ss"], at(1, 1))
                        root(b_rs[:], psum[2][:], b_rs[:], 1.0 / DK, "rs_qk")
                        act.copy(b_gb[:], projected(3))
                        split_act(act, u.ahead(5))
                        act.wait_ge(S["vt_mm"], at(1, 1))
                        act.copy(b_vt[:], psum[5][:, 0:L]).then_inc(S["vt_ready"], 1)
                        act.copy(b_gc[:], projected(4))
                        split_act(act, u.ahead(6))
                        act.wait_ge(S["sc_ready"], at(1, 1))
                        for m, (a, b) in enumerate(((0, L), (3 * P, 3 * P + L), (L, 3 * P), (3 * P + L, 6 * P))):
                            e = f(b_s[:, a:b], b_s[:, a:b], ACT.Exp, bias=b_st[:, m:m + 1], accum_out=b_st[:, 4 + m:5 + m])
                        e.then_inc(S["p_exp"], 1)
                        act.copy(b_ci[:], projected(5)).then_inc(S["gates_ready"], 1)
                        split_act(act, u.ahead(7))
                        act.wait_ge(S["pt_mm"], at(1, 1))
                        act.copy(b_pt[:], psum[6][:, 0:3 * P]).then_inc(S["pt_ready"], 1)
                        act.wait_ge(S["av_mm"], at(1, 1))
                        f(b_qs[:, 0:L], psum[7][:, 0:L], ACT.Square).then_inc(S["av_sq"], 1)
                        act.wait_ge(S["av_ss"], at(1, 1))
                        root(b_rs[:, L:2 * L], psum[2][:, 0:L], b_rs[:, 0:L], 1.0 / P, "av_rs")
                        tile = i * (2 * L) + j * L
                        act.wait_ge(S["conv_f32"], at(1, 1))
                        act.copy(a_hi[:, ds(tile + HEADS * L, L)], b_co[:]).then_inc(S["conv_hi"], 1)
                        act.wait_ge(S["attn_f32"], at(1, 1))
                        act.copy(a_hi[:, ds(tile, L)], b_o[:]).then_inc(S["attn_hi"], 1)
                own.end(HEADS // 2)
                with act.Fori(0, KT // 4) as i:
                    for j in range(4):
                        split_act(act, Unit(base + N_IN2 + j + 2, i))
                norm_root(2 + 2 * l)
                norm_hi(2 * l + 1)
                act.wait_ge(S["rel_out"], 32)
                c = base + N_IN2 + KT
                for kind, q in MLP_ORDER:
                    def turn_(i, j):
                        u = Unit(c + j, i)
                        if kind == "up":
                            at = (l * FQ + q) * KT + j + 1
                            act.wait_ge(unit_done, u.n + 1)
                            f(hbuf[:, (j % 2) * L:(j % 2) * L + L], psum[u.bank][:, 0:L], ACT.Relu).then_inc(S["relu_ready"], 1)
                            split_act(act, u.ahead(2))
                            act.wait_ge(S["sq_relu"], i * 4 + at)
                            tile = i * (4 * L) + ((q % 2) * KT + j) * L
                            act.copy(a_hi[:, ds(tile, L)], hbuf[:, (2 + j % 2) * L:(3 + j % 2) * L]).then_inc(S["hi_relu"], 1)
                        elif not isinstance(i, int) or u.c + i * 4 + 2 < N_UNITS:
                            split_act(act, u.ahead(2))
                    run(act, turn_, c + KT == N_UNITS)
                    c += KT

        @block.vector
        def _(dve):
            own = Chain(dve, S["dve_own"])
            tt, ts, stt = dve.tensor_tensor, dve.tensor_scalar, dve.scalar_tensor_tensor

            def conv(pad, acc, n, weight):
                own.link(ts(acc[:, 0:n], pad[:, 0:n], weight(0), None, ALU.mult))
                for k in range(1, TAPS):
                    m = stt(acc[:, 0:n], pad[:, k:k + n], weight(k), acc[:, 0:n], ALU.mult, ALU.add)
                    if k < TAPS - 1:
                        own.link(m)
                return m

            dve.wait_ge(S["c_silu"], 1)
            tt(d3(c4[:], 4)[:, :, 2:4], d3(cs[:], 2), d3(c4[:], 4)[:, :, 0:2], ALU.subtract).then_inc(S["c_ready"], 1)
            dve.wait_ge(S["rel_mm"], 1)
            dve.tensor_copy(by_dist[0:16, :], psum[5][0:16, 0:DIST]).then_inc(S["rel_copy"], 1)
            split_dve(dve, Unit(0))
            split_dve(dve, Unit(1))
            dve.wait_ge(S["rs1_ready"], 1)
            for q in range(4):
                x4 = d3(xr[:, q * 4 * T:(q + 1) * 4 * T], T)
                own.add(tt(x4, x4, over(rs1[:], 4), ALU.mult))
            with dve.Fori(0, 12) as i:
                for q in range(4):
                    split_dve(dve, Unit(q + 2, i))
            own.wait()
            dve.wait_ge(S["ada_cols"], 12)
            own.link(tt(d3(mods[:], 2), d3(psum[3][:, 0:96], 2), bc(par("b_ada", 0, 48), 2), ALU.add))
            own.link(stt(d3(coef[:], 2), d3(mods[:, 32:64], 2), 1.0, bc(par("pre", 0, KT), 2), ALU.add, ALU.mult))

            def low(k):
                dve.wait_ge(S["u_hi"], k + 1)
                tt(a_lo[:, k * T:(k + 1) * T], xr[:, k * T:(k + 1) * T], a_hi[:, k * T:(k + 1) * T],
                   ALU.subtract).then_inc(S["u_ready"], 1)
            for k in range(KT):
                for v in range(2):
                    x = xr[:, k * T + v * L:k * T + (v + 1) * L]
                    m = ts(x, x, coef[:, 2 * k + v:2 * k + v + 1], mods[:, 2 * k + v:2 * k + v + 1], ALU.mult, ALU.add)
                m.then_inc(S["u_f32"], 1)
                if k:
                    low(k - 1)
            low(KT - 1)
            leave(dve, 1)

            dve.wait_ge(unit_done, U_SMALL + 1)
            ts(sm[:], psum[0][:], par("sign"), par("dt_bias"), ALU.mult, ALU.add).then_inc(S["sm_lin"], 1)
            split_dve(dve, Unit(U_SMALL + 2))
            dve.wait_ge(S["sm_soft"], 1)
            own.add(stt(sm[:], sm[:], 0.0, sm_e[:], ALU.max, ALU.add))
            own.link(tt(gmul[:, 1:2], gmul[:, 0:1], par("mul"), ALU.mult))
            ts(sm_e[:], sm[:], gmul[:, 1:2], None, ALU.mult).then_inc(S["sm_mul"], 1)
            dve.wait_ge(S["sm_sums"], 1)
            cum3, tot3, end3, exp3, dec3 = (d3(a[:], 48) for a in (gcum, gtot, gend, gexp, gdec))
            for d in range(2):
                b = d3(psum[3][:, d * 192:d * 192 + 192], 48)
                dve.tensor_copy(cum3[:, :, d * 16:d * 16 + 16], b[:, :, d * 16:d * 16 + 16])
                own.add(dve.tensor_copy(cum3[:, :, 32 + d * 8:40 + d * 8], b[:, :, 32 + d * 8:40 + d * 8]))
            own.link(dve.tensor_copy(gtot[:], psum[4][:, 0:192]))
            tt(gend[:], gtot[:], gcum[:], ALU.subtract).then_inc(S["sm_cum"], 1)
            dve.wait_ge(S["sm_exp"], 1)
            tm3 = d3(tm[:], P)

            def head_cols(kind, k=0):
                return wk_g[:].rearrange("p (h k d c) -> p h k d c", k=6, d=2, c=C)[:, :, kind]

            def by_head(a):
                return a.rearrange("p c (d h) -> p h d c", d=2)

            def tile_cols(kind, d):
                return wk_s[:].rearrange("p (t k d c a) -> p t k d c a", k=5, d=2, c=C, a=2)[:, :, kind, d]

            def by_tile(a, d):
                return a.rearrange("p c (d t a) -> p t d c a", d=2, a=2)[:, :, d]
            for d in range(2):
                for kind, a in ((0, tm3[:, :, 32:48]), (1, cum3[:, :, 32:48]), (2, tm3[:, :, 64:80]), (4, end3[:, :, 32:48]),
                                (5, dec3[:, :, 32:48])):
                    dve.tensor_copy(head_cols(kind)[:, :, d], by_head(a)[:, :, d])
                tt(head_cols(3)[:, :, d], by_head(tm3[:, :, 64:80])[:, :, d], by_head(exp3[:, :, 32:48])[:, :, d], ALU.mult)
                for kind, a in ((0, tm3[:, :, 0:32]), (1, cum3[:, :, 0:32]), (2, tm3[:, :, 96:128]), (4, dec3[:, :, 0:32])):
                    dve.tensor_copy(tile_cols(kind, d), by_tile(a, d))
                tt(tile_cols(3, d), by_tile(tm3[:, :, 96:128], d), by_tile(end3[:, :, 0:32], d), ALU.mult)
            leave(dve, 2)
            dve.memset(g_S[:, 0:P], 0.0).then_inc(S["head_done"], 1)
            dve.memset(g_S[:, P:2 * P], 0.0).then_inc(S["tile_done"], 1)
            dve.wait_ge(S["ld_masks"], 16)

            def col(kind, d, c):
                k = kind * 8 + d * 4 + c
                return g_w[:, k:k + 1]

            def cols4(kind, d):
                return g_w[:, kind * 8 + d * 4:kind * 8 + d * 4 + 4]
            with dve.Fori(0, HG) as i:
                own.begin(i, 13)
                u = Unit(U_GDN, i)
                for j in range(3):
                    split_dve(dve, u.ahead(j + 2))
                    dve.wait_ge(S["pad_ready"], i * 3 + (j + 1))
                    conv(g_pad[j], g_acc[j], 520 if j else 262,
                         lambda k: par("conv_gdn", i * TAPS + (j * HG * TAPS + k))).then_inc(S["conv_done"], 1)
                dve.wait_ge(S["g_rows"], i + 1)
                dve.wait_ge(S["qkv_ready"], i + 1)
                for d in range(2):
                    for c in range(C):
                        b = (d * 4 + c) * P
                        stt(g_L[:, b:b + P], psum[6 + d][:, c * P:(c + 1) * P], col(1, d, c), K("pos", d), ALU.subtract, ALU.add)
                for d in range(2):
                    for c in range(2):
                        b = (d * 2 + c) * P
                        m = stt(g_A[:, b:b + P], psum[6 + d][:, c * P:(c + 1) * P], col(1, d, c), K("neg", d), ALU.subtract, ALU.add)
                m.then_inc(S["dpre"], 1)
                split_dve(dve, u.ahead(5))
                dve.wait_ge(S["gr_ready"], i + 1)
                tt(g_q[:], g_q[:], g_M[0][:, T:T + L], ALU.mult)
                tt(g_k[:], g_k[:], g_M[0][:, 0:T], ALU.mult).then_inc(S["kn_ready"], 1)
                dve.wait_ge(S["dexp"], i + 1)
                dve.wait_ge(S["gram"], i * 2 + 1)
                for d in range(2):
                    for c in range(C):
                        b = (d * 4 + c) * P
                        m = stt(g_L[:, b:b + P], psum[4][:, c * P:(c + 1) * P], col(2, d, c), g_L[:, b:b + P], ALU.mult, ALU.mult)
                m.then_inc(S["l_ready"], 1)
                dve.wait_ge(S["gram"], i * 2 + 2)
                for d in range(2):
                    tt(g_A[:, d * L:(d + 1) * L], g_A[:, d * L:(d + 1) * L], psum[5][:, 0:L], ALU.mult)
                for d in range(2):
                    m = tt(g_qd[:, d * L:(d + 1) * L], g_qd[:, d * L:(d + 1) * L], g_q[:], ALU.mult)
                m.then_inc(S["aq_ready"], 1)
                for d in range(2):
                    half = slice(d * 512, d * 512 + 512)
                    dve.wait_ge(S["x_mm"], i * 14 + (d + 1))
                    stt(d3(g_U[:, half], P), d3(psum[2 + d][:], P), -1.0, over(IDENT, 4), ALU.mult, ALU.add)
                    m = stt(d3(g_T[:, half], P), d3(g_M[0][:, half], P), -1.0, over(IDENT, 4), ALU.mult, ALU.add)
                m.then_inc(S["first_ut"], 1)
                for level in range(1, LEVELS):
                    for d in range(2):
                        dve.wait_ge(S["x_mm"], i * 14 + (2 * level + d + 1))
                        stt(d3(g_X[:, d * 512:d * 512 + 512], P), d3(psum[4 + d][:], P), -1.0, over(IDENT, 4),
                            ALU.mult, ALU.add).then_inc(S["xp_ready"], 1)
                for kind, out, bank, turn_ in ((3, g_kb, 2, 1), (4, g_ke, 2, 1), (2, g_vb, 3, 2)):
                    dve.wait_ge(S["nw_mm"], i * 4 + turn_)
                    for d in range(2):
                        m = tt(d3(out[:, d * 512:d * 512 + 512], P), d3(psum[bank][:], P), bc(cols4(kind, d), P), ALU.mult)
                    if kind != 4:
                        m.then_inc(S["tok_used"], 1)
                for step in range(3):
                    for d in range(2):
                        dve.wait_ge(S["s_mm"], i * 6 + (2 * step + d + 1))
                        s, add = g_S[:, d * P:(d + 1) * P], psum[2 + d][:, 0:P]
                        if step == 0:
                            m = dve.tensor_copy(s, add)
                        else:
                            m = stt(s, s, col(5, d, ORDER[d][step]), add, ALU.mult, ALU.add)
                        m.then_inc(S["s_ready"], 1)
                dve.wait_ge(S["o_rs"], i + 1)
                own.link(stt(g_X[:, L:2 * L], psum[4][:, 0:L], par("gdn_norm"), g_M[0][:, L:2 * L], ALU.mult, ALU.mult))
                z = x_res[:, ds(i * L + HG * L, L)]
                tt(z, z, g_X[:, L:2 * L], ALU.mult).then_inc(S["head_done"], 1)
            own.end(HG)

            leave(dve, 3)
            dve.wait_ge(S["pads_set"], 2)
            for j in range(4):
                split_dve(dve, Unit(U_BC + j + 2))
                dve.wait_ge(S["bc_pad"], j + 1)
                if j:
                    dve.wait_ge(S["bc_ready"], j)
                conv(s_pad, s_acc, 520 if j < 2 else 262,
                     lambda k: par("conv_ssd", (8 + j) * TAPS + k)).then_inc(S["bc_conv"], 1)
            dve.wait_ge(S["bc_tok"], 1)
            for g in range(2):
                with dve.Fori(0, 2) as i:
                    own.begin(i, 2 * 11)
                    for a in range(2):
                        t = g * 4 + a
                        u = Unit(U_SSD + 2 * t, i)
                        split_dve(dve, u.ahead(2))
                        dve.wait_ge(S["sx_pad"], i * 2 + (t + 1))
                        conv(s_pad, s_acc, 520, lambda k: par("conv_ssd", i * (2 * TAPS) + (t * TAPS + k))).then_inc(S["sx_conv"], 1)
                        dve.wait_ge(S["s_rows"], i * 2 + (t + 1))
                        for d in range(2):
                            for e in range(4):
                                b = (d * 4 + e) * P
                                k = 16 + d * 8 + e
                                m = stt(s_M[:, b:b + P], psum[3 + d][:, e * P:(e + 1) * P], s_w[:, k:k + 1], K("neg", d),
                                        ALU.subtract, ALU.add)
                        m.then_inc(S["s_pre"], 1)
                        split_dve(dve, u.ahead(3))
                        dve.wait_ge(S["s_tok"], i * 2 + (t + 1))
                        for d in range(2):
                            m = tt(d3(s_de[:, d * T:(d + 1) * T], 64), d3(psum[2][:], 64), bc(s_w[:, 48 + d * 8:56 + d * 8], 64), ALU.mult)
                        m.then_inc(S["s_de_ready"], 1)
                        for d in range(2):
                            tt(d3(s_dt[:, d * L:(d + 1) * L], 64), d3(psum[2][:, 0:L], 64), bc(s_w[:, 32 + d * 8:36 + d * 8], 64), ALU.mult)
                        dve.wait_ge(S["st_mm"], i * 2 + (t + 1))
                        for d in range(2):
                            own.add(dve.tensor_copy(s_H[:, d * 3 * P:(d * 3 + 1) * P], psum[5 + d][:, 0:P]))
                        for n in (1, 2):
                            own.wait()
                            for d in range(2):
                                for e in range(2):
                                    at = (d * 3 + n) * P + e * 64
                                    k = 64 + d * 8 + ORDER[d][n] * 2 + e
                                    m = stt(s_H[:, at:at + 64], s_H[:, at - P:at - P + 64], s_w[:, k:k + 1],
                                            psum[5 + d][:, n * P + e * 64:n * P + e * 64 + 64], ALU.mult, ALU.add)
                                    if n == 1:
                                        own.add(m)
                        m.then_inc(S["h_ready"], 1)
                        dve.wait_ge(S["s_exp"], i * 2 + (t + 1))

                        def four(ap, d):
                            return ap[:, d * T:(d + 1) * T].rearrange("p (c a q) -> p c a q", c=2, a=2)

                        def pair(ap):
                            return d3(ap, P).unsqueeze(2).broadcast_to([P, 2, 2, P])
                        for d in range(2):
                            tt(four(s_M[:], d), four(s_M[:], d), pair(s_cb[:, g * L:(g + 1) * L]), ALU.mult)
                            m = tt(four(s_C[:], d), four(s_C[:], d), pair(s_ct[:, g * L:(g + 1) * L]), ALU.mult)
                        m.then_inc(S["s_mc_ready"], 1)
                        dve.wait_ge(S["y_mm"], i * 2 + (t + 1))
                        own.link(stt(s_y[:], s_x[:, 0:L], par("skip", i * 2 + t), psum[7][:, 0:L], ALU.mult, ALU.add))
                        z = x_res[:, ds(i * (2 * L) + t * L, L)]
                        tt(z, z, s_y[:], ALU.mult).then_inc(S["tile_done"], 1)
                own.end(2)
                dve.wait_ge(S["grp_rs"], g + 1)
                for k in range(4):
                    x = x_res[:, (g * 4 + k) * L:(g * 4 + k + 1) * L]
                    stt(x, x, par("ssd_norm", g * 4 + k), s_y[:], ALU.mult, ALU.mult)
            leave(dve, 4)

            for q in range(4):
                dve.wait_ge(S["y_hi"], q + 1)
                x = slice(q * 1024, (q + 1) * 1024)
                tt(a_lo[:, x], x_res[:, x], a_hi[:, x], ALU.subtract).then_inc(S["y_ready"], 1)
            lam = d3(par("lam", 0, LAYERS * 4 * DK), DK)
            own.link(tt(d3(b_s[:, 0:4 * DK], DK), lam[:, 0:8:2], lam[:, 1:8:2], ALU.mult))
            dve.tensor_reduce(small[:, 16:20], d3(b_s[:, 0:4 * DK], DK), AX.X, ALU.add).then_inc(S["lam_d"], 1)
            dve.memset(b_cm[:, 0:1], 0.0).then_inc(S["mlp_ready"], 1)
            dve.memset(b_cm[:, 1:2], 0.0).then_inc(S["mlp_ready"], 1)
            own.add(tt(small[:, 0:KT], mods[:, 64:96:2], par("post", 0, KT), ALU.mult))
            for l in range(LAYERS):
                own.add(ts(small[:, 26 + l:27 + l], par("subln", l), 1.0 - lam_init(l), None, ALU.mult))
            with dve.Fori(0, KT // 4) as i:
                for j in range(4):
                    split_dve(dve, Unit(U_WOUT + j + 2, i))
            own.wait()
            dve.wait_ge(S["x_loaded"], 16)
            dve.wait_ge(S["rs_ready"], 1)

            def gated(k):
                own.add(stt(hbuf[:, (k % 4) * L:(k % 4 + 1) * L], mo[:, k * L:(k + 1) * L], small[:, k:k + 1], n_rs[:],
                            ALU.mult, ALU.mult))
            gated(0)
            for k in range(KT):
                own.wait()
                if k + 1 < KT:
                    gated(k + 1)
                x = x_res[:, k * L:(k + 1) * L]
                tt(x, x, hbuf[:, (k % 4) * L:(k % 4 + 1) * L], ALU.add).then_inc(S["sx_upd"], 1)
            dve.wait_ge(S["lam_e"], 1)
            own.link(tt(small[:, 24:26], small[:, 21:24:2], small[:, 20:24:2], ALU.subtract))
            for l in range(LAYERS):
                own.add(ts(small[:, 24 + l:25 + l], small[:, 24 + l:25 + l], -lam_init(l), None, ALU.add))

            def norm(e, name, l):
                dve.wait_ge(S["rs_ready"], e + 2)

                def low(g):
                    dve.wait_ge(S["h_hi_ready"], e * 8 + g + 1)
                    tt(h_lo[:, g * T:(g + 1) * T], hbuf[:, (g % 2) * T:(g % 2) * T + T], h_hi[:, g * T:(g + 1) * T],
                       ALU.subtract).then_inc(S["h_ready2"], 1)
                for g in range(8):
                    if g >= 2:
                        dve.wait_ge(S["h_ready2"], e * 8 + g - 1)
                    for k in range(2 * g, 2 * g + 2):
                        m = stt(hbuf[:, (k % 4) * L:(k % 4 + 1) * L], x_res[:, k * L:(k + 1) * L], par(name, l * KT + k), n_rs[:],
                                ALU.mult, ALU.mult)
                    m.then_inc(S["h_f32"], 1)
                    if g:
                        low(g - 1)
                low(7)

            for l in range(LAYERS):
                base = U_LAYER + l * N_LAYER
                dve.wait_ge(S["sx_upd"], (2 * l + 1) * KT)
                norm(2 * l, "attn_norm", l)
                if l:
                    dve.wait_ge(S["bias_ready"], 16)
                with dve.Fori(0, HEADS // 2) as i:
                    own.begin(i, 2 * 13)
                    for j in range(2):
                        def at(n, k):
                            return i * (2 * n) + ((l * HEADS + j) * n + k)
                        u = Unit(base + 6 * j, i, 3)
                        for m in range(3):
                            split_dve(dve, u.ahead(m + 2))
                        dve.wait_ge(S["rs_qk"], at(1, 1))
                        for m, name in enumerate(("qg", "kg")):
                            x = b_qk[:, m * L:(m + 1) * L]
                            s = stt(x, x, par(name, l), b_rs[:, m * L:(m + 1) * L], ALU.mult, ALU.mult)
                        s.then_inc(S["qk_ready"], 1)
                        split_dve(dve, u.ahead(5))
                        dve.wait_ge(S["score_mm"], at(1, 1))
                        b = bias[:, ds(i * (4 * L) + j * 2 * L, 2 * L)]
                        for m in range(2):
                            s = m * 3 * P
                            own.add(stt(b_s[:, s:s + L], psum[3 + m][:, 0:L], DK ** -0.5, b[:, m * L:(m + 1) * L], ALU.mult, ALU.add))
                            own.add(stt(b_s[:, s + L:s + 3 * P], psum[3 + m][:, L:L + P], DK ** -0.5, b[:, m * L + P:(m + 1) * L],
                                        ALU.mult, ALU.add))
                        own.wait()
                        parts = d3(b_s, 3 * P)
                        dve.tensor_reduce(b_st[:, 0:2], parts[:, :, 0:L], AX.X, ALU.max, negate=True)
                        dve.tensor_reduce(b_st[:, 2:4], parts[:, :, L:3 * P], AX.X, ALU.max, negate=True).then_inc(S["sc_ready"], 1)
                        split_dve(dve, u.ahead(6))
                        dve.wait_ge(S["p_exp"], at(1, 1))
                        own.link(dve.reciprocal(b_st[:, 8:12], b_st[:, 4:8]))
                        own.add(ts(b_st[:, 9:12:2], b_st[:, 9:12:2], small[:, 24 + l:25 + l], None, ALU.mult))
                        own.add(ts(b_s[:, 0:L], b_s[:, 0:L], b_st[:, 8:9], None, ALU.mult))
                        own.link(ts(b_s[:, L:3 * P], b_s[:, L:3 * P], b_st[:, 10:11], None, ALU.mult))
                        stt(b_s[:, 0:L], b_s[:, 3 * P:3 * P + L], b_st[:, 9:10], b_s[:, 0:L], ALU.mult, ALU.add)
                        stt(b_s[:, L:3 * P], b_s[:, 3 * P + L:6 * P], b_st[:, 11:12], b_s[:, L:3 * P], ALU.mult, ALU.add
                            ).then_inc(S["p_ready"], 1)
                        split_dve(dve, u.ahead(7))
                        dve.wait_ge(S["gates_ready"], at(1, 1))
                        w = [par("conv2", i * 6 + ((l * HEADS + j) * 3 + k)) for k in range(3)]
                        own.link(tt(b_cm[:, 2:2 + L], b_gc[:], b_ci[:], ALU.mult))
                        own.link(ts(b_co[:], b_cm[:, 2:2 + L], w[2], None, ALU.mult))
                        own.link(stt(b_co[:], b_cm[:, 1:1 + L], w[1], b_co[:], ALU.mult, ALU.add))
                        own.link(stt(b_co[:], b_cm[:, 0:L], w[0], b_co[:], ALU.mult, ALU.add))
                        own.link(tt(b_co[:], b_co[:], b_gb[:], ALU.mult))
                        dve.nop().then_inc(S["conv_f32"], 1)
                        tile = i * (2 * L) + j * L
                        dve.wait_ge(S["av_rs"], at(1, 1))
                        stt(b_o[:], psum[7][:, 0:L], small[:, 26 + l:27 + l], b_rs[:, L:2 * L], ALU.mult, ALU.mult
                            ).then_inc(S["attn_f32"], 1)
                        dve.wait_ge(S["conv_hi"], at(1, 1))
                        y = ds(tile + HEADS * L, L)
                        tt(a_lo[:, y], b_co[:], a_hi[:, y], ALU.subtract).then_inc(S["yt_ready"], 1)
                        dve.wait_ge(S["attn_hi"], at(1, 1))
                        y = ds(tile, L)
                        tt(a_lo[:, y], b_o[:], a_hi[:, y], ALU.subtract).then_inc(S["yt_ready"], 1)
                own.end(HEADS // 2)

                def add_to_x(i, c, j, signal):
                    u = Unit(c + j, i)
                    dve.wait_ge(unit_done, u.n + 1)
                    x = x_res[:, ds(i * (4 * L) + j * L, L)]
                    m = tt(x, x, psum[u.bank][:, 0:L], ALU.add)
                    if signal:
                        m.then_inc(S[signal], 1)
                    if not isinstance(i, int) or u.c + i * 4 + 2 < N_UNITS:
                        split_dve(dve, u.ahead(2))
                with dve.Fori(0, KT // 4) as i:
                    for j in range(4):
                        add_to_x(i, base + N_IN2, j, "sx_upd")
                dve.wait_ge(S["sx_upd"], (2 * l + 2) * KT)
                norm(2 * l + 1, "mlp_norm", l)
                c = base + N_IN2 + KT
                for kind, q in MLP_ORDER:
                    def turn_(i, j):
                        if kind == "up":
                            u = Unit(c + j, i)
                            split_dve(dve, u.ahead(2))
                            dve.wait_ge(S["hi_relu"], i * 4 + ((l * FQ + q) * KT + j + 1))
                            tile = ds(i * (4 * L) + ((q % 2) * KT + j) * L, L)
                            tt(a_lo[:, tile], hbuf[:, (2 + j % 2) * L:(3 + j % 2) * L], a_hi[:, tile], ALU.subtract
                               ).then_inc(S["mlp_ready"], 1)
                        else:
                            add_to_x(i, c, j, None if q < 3 else "sx_upd" if l + 1 < LAYERS else "x_final")
                    run(dve, turn_, c + KT == N_UNITS)
                    c += KT


def lam_init(l):
    return 0.8 - 0.6 * math.exp(-0.3 * l)


def run(eng, turn, last):
    with eng.Fori(0, 3 if last else 4) as i:
        for j in range(4):
            turn(i, j)
    if last:
        for j in range(4):
            turn(3, j)


def columns(w):
    n = w.shape[1] // P
    return w.reshape(KT, P, n, P).transpose(2, 1, 0, 3).reshape(n, P, D)


def kernel(**inputs):
    import concourse.bacc as bacc
    from concourse.bass_utils import run_bass_kernel_spmd

    a = {k: np.ascontiguousarray(v) for k, v in inputs.items()}
    w_in, w_ada = a["w_in"][0], a["w_ada"][0]
    xbc, dt = 2048, 2048 + 1536
    qkv = dt + 32
    beta = qkv + 3072
    alpha = beta + 16
    none = np.zeros((D, 16), np.float32)
    small = np.concatenate([w_in[:, dt:qkv], w_in[:, alpha:alpha + 16], none, w_in[:, beta:beta + 16], none,
                            w_in[:, dt:qkv]], axis=1)
    z, x, bc = columns(w_in[:, 0:2048]), columns(w_in[:, xbc:xbc + 1024]), columns(w_in[:, xbc + 1024:dt])
    qkv_u = columns(w_in[:, qkv:beta])
    parts = [w_ada.reshape(4, 4, P, 12, 512).transpose(3, 0, 2, 1, 4).reshape(48, P, D), columns(small)]
    parts += [np.stack([qkv_u[h], qkv_u[HG + h], qkv_u[2 * HG + h], z[TS + h]]) for h in range(HG)]
    parts += [bc]
    parts += [np.stack([x[t], z[t]]) for t in range(TS)]
    parts += [columns(a["w_out"][0])]
    for l in range(LAYERS):
        w2 = columns(a["w_in_2"][l])
        parts += [w2[[h + 8 * k for k in range(6)]] for h in range(HEADS)]
        parts += [columns(a["w_out_2"][l])]
        for kind, q in MLP_ORDER:
            if kind == "up":
                parts += [columns(a["w_up_2"][l][:, q * D:(q + 1) * D])]
            else:
                parts += [columns(a["w_down_2"][l][q * D:(q + 1) * D])]
    stream = np.concatenate(parts)
    assert stream.shape == (N_UNITS, P, D)

    def feat(v):
        return np.ascontiguousarray(v.reshape(-1, P).T)

    pars = np.zeros((P, N_PAR), np.float32)

    def par(name, v):
        at, w = PAR[name]
        assert v.shape == (P, w), (name, v.shape)
        pars[:, at:at + w] = v
    par("c", np.stack([a["c"].reshape(KT, P).T, a["c_ctx"].reshape(KT, P).T], axis=2).reshape(P, 2 * KT))
    par("b_ada", feat(a["b_ada"]))
    par("pre", feat(a["pre_norm_w"]))
    par("post", feat(a["post_norm_w"]))
    par("conv_ssd", a["conv_ssd_w"].reshape(TAPS, 12, P).transpose(2, 1, 0).reshape(P, -1))
    par("bias_ssd", feat(a["conv_ssd_b"]))
    par("conv_gdn", a["conv_gdn_w"].reshape(TAPS, 24, P).transpose(2, 1, 0).reshape(P, -1))
    rows = np.zeros((4, P), np.float32)
    rows[0] = 1.0
    rows[0, 64:96] = -1.0
    rows[1, 0:32] = rows[1, 96:128] = a["ssd_dt_bias"].reshape(-1)
    rows[1, 32:48] = a["gdn_dt_bias"].reshape(-1)
    rows[2, 0:32] = a["ssd_a_log"].reshape(-1)
    rows[2, 32:48] = a["gdn_a_log"].reshape(-1)
    rows[3] = 1.0
    rows[3, 0:48] = -1.0
    for k, name in enumerate(("sign", "dt_bias", "a_log", "mul")):
        par(name, rows[k][:, None])
    par("skip", feat(np.repeat(a["ssd_d"].reshape(-1), 64)))
    par("ssd_norm", feat(a["ssd_norm_w"]))
    par("gdn_norm", feat(a["gdn_norm_w"]))
    par("attn_norm", feat(a["attn_norm_g_2"]))
    par("mlp_norm", feat(a["mlp_norm_g_2"]))
    par("conv2", a["conv_w_2"].reshape(LAYERS, 3, HEADS, P).transpose(3, 0, 2, 1).reshape(P, -1))
    par("qg", np.tile(a["q_norm_g_2"], (1, 2)).T)
    par("kg", np.tile(a["k_norm_g_2"], (1, 2)).T)
    par("subln", a["subln_g_2"].T)
    lam = np.stack([a[f"lambda_{n}_2"] for n in ("q1", "k1", "q2", "k2")], axis=1)
    par("lam", np.broadcast_to(lam.reshape(1, -1), (P, lam.size)))
    x_t = np.ascontiguousarray(np.concatenate([a["x"][0], a["ctx"][0]]).T)

    nc = bacc.Bacc("TRN2", target_bir_lowering=False, num_devices=1)
    arrays = {"stream": stream, "x_t": x_t, "const": constants(), "buckets": bucket_rows(), "pars": pars, "rel": a["rel_bias_2"]}
    handles = [nc.dram_tensor(k, v.shape, F32, kind="ExternalInput").ap() for k, v in arrays.items()]
    out = nc.dram_tensor("out_t", (D, L), F32, kind="ExternalOutput").ap()
    scratch = [nc.dram_tensor("by_distance", (2 * HEADS, DIST), F32, kind="Internal").ap(),
               nc.dram_tensor("bias_table", (P, 2 * HEADS * L), F32, kind="Internal").ap()]
    build(nc, *handles, out, scratch)
    r = run_bass_kernel_spmd(nc, [arrays], core_ids=[0])
    return np.ascontiguousarray(r.results[0]["out_t"].T).reshape(1, L, D)
```

```python
import math

import numpy as np
import concourse.bass as bass
from concourse import mybir
from contextlib import ExitStack

F32 = mybir.dt.float32
F32R = mybir.dt.float32r
ACT = mybir.ActivationFunctionType
ALU = mybir.AluOpType
AX = mybir.AxisListType
ds = bass.ds

P = 128
D = 2048
KT = D // P
L = 256
T = 512
C = T // P
ROW = 64
HG = 8
TS = 8
TAPS = 5
EPS = 1e-6
BIG = 1e30
LEVELS = 7
HEADS = 8
DK = 64
BUCKETS = 32
LAYERS = 2
LOG_EXP = "natural_log_exp_and_others"
FQ = 4

U_ADA = 0
U_SMALL = 48
U_GDN = U_SMALL + 1
U_BC = U_GDN + 4 * HG
U_SSD = U_BC + 4
U_WOUT = U_SSD + 2 * TS
U_LAYER = U_WOUT + KT
N_IN2 = 6 * HEADS
N_LAYER = N_IN2 + KT + 2 * FQ * KT
N_UNITS = U_LAYER + LAYERS * N_LAYER
RAW = 4
SPL = 2

EARLY = 8

CONST = {"ident": 0, "ones": P, "flip": 2 * P, "blk": 3 * P, "sel": 4 * P}
KEEP = 4 * P + 8
CONST.update({"tri": KEEP, "pos": KEEP + 2 * P, "neg": KEEP + 4 * P, "level": KEEP + 6 * P})
N_CONST = KEEP + (6 + 2 * LEVELS) * P
DIST = 384

PAR, _at = {}, 0
for _name, _w in (("c", 2 * KT), ("b_ada", 48), ("pre", KT), ("post", KT), ("conv_ssd", 12 * TAPS), ("bias_ssd", 12),
                  ("conv_gdn", 24 * TAPS), ("sign", 1), ("dt_bias", 1), ("a_log", 1), ("mul", 1), ("skip", TS),
                  ("ssd_norm", TS), ("gdn_norm", 1), ("attn_norm", LAYERS * KT), ("mlp_norm", LAYERS * KT),
                  ("conv2", LAYERS * HEADS * 3), ("qg", LAYERS), ("kg", LAYERS), ("subln", LAYERS),
                  ("lam", LAYERS * 4 * DK)):
    PAR[_name] = (_at, _w)
    _at += _w
N_PAR = _at

PADW = 4 * (ROW + 2) + 2
PADT = PADW + L + 2
MLP_ORDER = (("up", 0), ("up", 1), ("down", 0), ("up", 2), ("down", 1), ("up", 3), ("down", 2), ("down", 3))
FILL = (None, (1, 9, 13), (1, 13, KT), (2, 0, 5), (2, 5, 11), (2, 11, KT))
ORDER = (("up", 0), ("up", 1), ("down", 0), ("up", 2), ("down", 1), ("up", 3), ("down", 2), ("down", 3))
FILL = (None, (1, 9, 13), (1, 13, KT), (2, 0, 5), (2, 5, 11), (2, 11, KT))
KINDS_G = ("raw", "cum", "beta", "kb", "end", "dec")
KINDS_S = ("raw", "cum", "dt", "dte", "dec")
ORDER = ((2, 3, 0, 1), (3, 2, 1, 0))


def constants():
    i, j = np.arange(P)[:, None], np.arange(P)[None, :]
    out = np.zeros((P, N_CONST), np.float32)

    def put(name, k, a):
        at = CONST[name] + k * P
        out[:, at:at + P] = a
    put("ident", 0, i == j)
    put("ones", 0, 1.0)
    put("flip", 0, i + j == P - 1)
    put("blk", 0, i // DK == j // DK)
    for r in range(4):
        out[r, CONST["sel"] + r % 2] = 1.0
    for d in range(2):
        le = i <= j if d == 0 else i >= j
        lt = j < i if d == 0 else j > i
        put("tri", d, le)
        put("pos", d, np.where(lt, 0.0, BIG))
        put("neg", d, np.where(le, 0.0, -BIG))
        for level in range(LEVELS):
            s = 1 << level
            a, b = (i, j) if d == 0 else (j, i)
            put("level", d * LEVELS + level,
                (a // (2 * s) == b // (2 * s)) & (a // s % 2 == 1) & (b // s % 2 == 0))
    return out


def bucket_rows():
    dist = 255 - np.arange(DIST)
    n = np.maximum(dist, 0)
    exact = BUCKETS // 2
    nf = np.maximum(n, exact).astype(np.float32)
    ratio = np.log(nf / np.float32(exact)) / np.float32(math.log(128 / exact))
    large = exact + (ratio * np.float32(BUCKETS - exact)).astype(np.int32)
    bucket = np.where(n < exact, n, np.minimum(large, BUCKETS - 1))
    bucket = np.where(dist < 0, BUCKETS, bucket)
    return (np.arange(BUCKETS + 1)[:, None] == bucket[None, :]).astype(np.float32)


class Unit:

    def __init__(self, c, i=0, groups=1):
        self.c, self.i, self.groups = c, i, groups
        self.n = c + i * (4 * groups)
        self.raw = c % RAW
        self.turn = c // RAW + i * groups
        self.slot = c % SPL
        self.bank = c % 2

    def ahead(self, k):
        return Unit(self.c + k, self.i, self.groups)


class Chain:

    def __init__(self, eng, sem):
        self.eng, self.sem, self.base, self.n = eng, sem, 0, 0

    def begin(self, i, per, start=0):
        self.before, self.per = self.base + self.n, per
        self.base, self.n = i * per + (self.before - start * per), 0

    def end(self, turns):
        assert self.n == self.per, f"{self.n} counted instructions in a turn, not {self.per}"
        self.base, self.n = self.before + turns * self.per, 0

    def add(self, instruction):
        instruction.then_inc(self.sem, 1)
        self.n += 1

    def wait(self):
        self.eng.wait_ge(self.sem, self.base + self.n)

    def link(self, instruction):
        self.add(instruction)
        self.wait()


def build(nc, stream, x_dram, const_dram, bucket_dram, par_dram, rel_dram, out_dram, scratch):
    ctx = ExitStack()
    with ctx:
        def sem(name):
            return ctx.enter_context(nc.semaphore(name))

        arena = ctx.enter_context(nc.sbuf_tensor("arena", [P, 53200], F32))
        top = {"at": 0}

        def put(name, cols, dt=F32, at=None):
            if at is None:
                at = top["at"]
                top["at"] = at + 4 * cols
            assert at + 4 * cols <= 4 * 53200, (name, at + 4 * cols - 4 * 53200)
            assert at % 32 == 0, (name, at)
            return nc.alloc_sbuf_tensor_at(name, [P, cols], dt, offset=ARENA0 + at)

        ARENA0 = nc.sbuf_base - 4 * 53200
        raw = [put(f"raw{r}", D) for r in range(RAW)]
        w_hi = [put(f"w_hi{s}", D, F32R) for s in range(SPL)]
        w_lo = [put(f"w_lo{s}", D, F32R) for s in range(SPL)]
        a_hi = put("a_hi", KT * T, F32R)
        a_lo = put("a_lo", KT * T, F32R)
        X_RES = top["at"]
        x_res = put("x_res", KT * L)
        relb = put("relb", 16, at=4 * (RAW * D + 2 * SPL * D + 2 * KT * T))
        onehot = put("onehot", DIST, at=4 * (RAW * D + 2 * SPL * D + 2 * KT * T + 16))
        by_dist = put("by_dist", DIST, at=4 * (RAW * D + 2 * SPL * D + 2 * KT * T + 16 + DIST))
        keep = put("keep", KEEP)
        pars = put("pars", (N_PAR + 7) // 8 * 8)
        mods = put("mods", 96)
        cols = put("cols", 8)
        shared = top["at"]
        masks = put("masks", N_CONST - KEEP)
        wk_g = put("wk_g", HG * 48)
        wk_s = put("wk_s", TS * 80)
        scans = top["at"]
        xr = put("xr", KT * T)
        xsq = put("xsq", 2 * T)
        rs1 = put("rs1", T)
        ln1 = put("ln1", T)
        mrow = put("mrow", 512)
        cs = put("cs", 2 * KT)
        c4 = put("c4", 4 * KT, F32R)
        coef = put("coef", 2 * KT)
        top["at"] = scans
        sm = put("sm", T)
        sm_e = put("sm_e", T)
        tm = put("tm", C * P)
        gcum, gtot, gend, gexp, gdec = (put(n, C * 48) for n in ("gcum", "gtot", "gend", "gexp", "gdec"))
        gmul = put("gmul", 8)
        top["at"] = scans
        g_pad = [put(f"g_pad{j}", w) for j, w in enumerate((272, 528, 528))]
        g_acc = [put(f"g_acc{j}", w, at=X_RES + 4 * a) for j, (w, a) in enumerate(((264, 0), (520, 264), (520, 784)))]
        g_A = put("g_A", 4 * P)
        g_qd = put("g_qd", 4 * P)
        g_q = put("g_q", L)
        g_k = put("g_k", T)
        g_v = put("g_v", T)
        g_w = put("g_w", 48)
        g_L = put("g_L", 8 * P)
        g_M = [put(f"g_M{j}", 8 * P) for j in range(2)]
        g_X = put("g_X", 8 * P)
        g_U = put("g_U", 8 * P)
        g_T = put("g_T", 8 * P)
        g_kb, g_ke, g_vb = g_X, g_M[0], g_M[1]
        g_vn = put("g_vn", 2 * P)
        g_S = put("g_S", 2 * P)
        top["at"] = scans
        s_pad = put("s_pad", 528)
        s_acc = put("s_acc", 520)
        s_bt = put("s_bt", 2 * T)
        s_ct = put("s_ct", 2 * L)
        s_btok = put("s_btok", 2 * T)
        s_cb = put("s_cb", 2 * L)
        s_x = [put(f"s_x{j}", T) for j in range(2)]
        s_w = put("s_w", 80)
        s_dt = put("s_dt", 2 * L)
        s_de = put("s_de", 2 * T)
        s_M = put("s_M", 8 * P)
        s_C = put("s_C", 8 * P)
        s_H = put("s_H", 6 * P)
        s_y = put("s_y", L)
        s_r = put("s_r", L)
        top["at"] = shared
        h_hi = put("h_hi", KT * L, F32R)
        turned = put("turned", KT * L, at=shared)
        h_lo = put("h_lo", KT * L, F32R)
        mo = put("mo", KT * L, at=shared + 4 * KT * L)
        bias = put("bias", 2 * HEADS * L, at=4 * (RAW * D + 2 * SPL * D + KT * L))
        n_sq, n_acc, n_ln, n_rs = (put(n, L) for n in ("n_sq", "n_acc", "n_ln", "n_rs"))
        hbuf = put("hbuf", 4 * L)
        small = put("small", 64)
        b_qk = put("b_qk", 2 * L)
        b_qs = put("b_qs", 2 * L)
        b_rs = put("b_rs", 2 * L)
        b_v = put("b_v", L)
        b_vt = put("b_vt", L)
        b_gb = put("b_gb", L)
        b_gc = put("b_gc", L)
        b_ci = put("b_ci", L)
        b_cm = put("b_cm", L + 8)
        b_co = put("b_co", L)
        b_pt = put("b_pt", 3 * P)
        b_o = put("b_o", L)
        b_s = hbuf[:, 0:768]
        b_st = put("b_st", 16)
        b_os, b_ol, b_or = n_sq, n_ln, n_rs
        psum = [ctx.enter_context(nc.psum_tensor(f"bank{k}", [P, 512], F32)) for k in range(8)]

        def K(name, k=0, w=P):
            at = CONST[name] + k * P
            return keep[:, at:at + w] if at < KEEP else masks[:, at - KEEP:at - KEEP + w]

        def par(name, k=0, w=1):
            at = PAR[name][0]
            return pars[:, ds(at + k, w)] if not isinstance(k, int) else pars[:, at + k:at + k + w]

        IDENT, ONES = K("ident"), K("ones")
        EPS_C, QS_C, ONE_C, ZERO_C = (cols[:, k:k + 1] for k in range(4))

        raw_ready = [sem(f"raw_ready{r}") for r in range(RAW)]
        hi_ready, lo_ready, unit_done = sem("hi_ready"), sem("lo_ready"), sem("unit_done")
        names = """ld_par ld_x ld_masks ld_rel half_hi cols_set c_silu c_ready sq1 x_sq x_sq_used ss1 rs1_ready xr_ready
            mrow_ready ada_cols u_f32 u_hi u_ready sm_lin sm_soft sm_mul sm_beta sm_turned tm_ready sm_sums
            sm_cum sm_exp left pads_set pad_ready conv_done gw_ready g_rows g_ss sq_ready gr_ready kn_ready gram
            dpre dexp tok_used l_ready aq_ready m_ready x_mm xp_ready first_ut uu_mm ut_ready nw_mm nw_ready
            vn_mm vn_ready s_mm s_ready o_mm osq_ready oss o_rs head_done bc_pad bc_conv bc_ready b_turned
            bc_tok sx_pad sx_conv sx_ready sw_ready s_rows s_tok s_pre s_exp s_de_ready s_mc_ready st_mm h_ready
            y_mm tile_done grp_sq grp_ss grp_rs y_hi y_ready mo_ready acc_ready turned_ready flip_mm flip_read
            rel_mm rel_copy rel_out x_loaded ss_mm rs_ready h_f32 h_hi_ready h_ready2 lam_e lam_d qk_sq rs_qk
            qk_ready qk_ss score_mm v_ready vt_mm vt_ready gates_ready sc_ready p_exp p_ready pt_mm pt_ready
            av_mm av_sq av_ss av_rs attn_f32 attn_hi conv_f32 conv_hi yt_ready sx_upd relu_ready sq_relu hi_relu
            mlp_ready x_final out_done rel_set bias_ready dve_own act_own pool_own""".split()
        S = {n: sem(n) for n in names}

        def split_act(act, u):
            act.wait_ge(raw_ready[u.raw], (u.turn + 1) * 16)
            if u.c >= SPL:
                act.wait_ge(unit_done, u.n - SPL + 1)
            act.copy(w_hi[u.slot][:], raw[u.raw][:]).then_inc(hi_ready, 1)

        def split_dve(dve, u):
            dve.wait_ge(hi_ready, u.n + 1)
            dve.tensor_tensor(w_lo[u.slot][:], raw[u.raw][:], w_hi[u.slot][:], ALU.subtract).then_inc(lo_ready, 1)

        def split_act_halves(act, u):
            act.wait_ge(raw_ready[u.raw], (u.turn + 1) * 16)
            if u.c >= SPL:
                act.wait_ge(unit_done, u.n - SPL + 1)
            act.copy(w_hi[u.slot][:, 0:D // 2], raw[u.raw][:, 0:D // 2]).then_inc(S["half_hi"], 1)
            act.copy(w_hi[u.slot][:, D // 2:D], raw[u.raw][:, D // 2:D]).then_inc(hi_ready, 1)

        def split_dve_halves(dve, u):
            for half, ready in ((slice(0, D // 2), S["half_hi"]), (slice(D // 2, D), hi_ready)):
                dve.wait_ge(ready, u.n + 1)
                m = dve.tensor_tensor(w_lo[u.slot][:, half], raw[u.raw][:, half], w_hi[u.slot][:, half], ALU.subtract)
            m.then_inc(lo_ready, 1)

        def unit_mm(pe, u, hi, lo, n, comes=None, order=None, part=(0, KT)):
            if part[0] == 0:
                pe.wait_ge(lo_ready, u.n + 1)
            acc = psum[u.bank][:, 0:n]
            first, final = (order[0], order[-1]) if order else (0, KT - 1)
            for k in order or range(*part):
                if comes and k in comes[1]:
                    pe.wait_ge(comes[0], comes[1][k])
                wh, wl = (w[u.slot][:, k * P:(k + 1) * P] for w in (w_hi, w_lo))
                pe.matmul(acc, wh, lo[:, k, 0:n], start=(k == first), stop=False)
                pe.matmul(acc, wl, hi[:, k, 0:n], start=False, stop=False)
                last = pe.matmul(acc, wh, hi[:, k, 0:n], start=False, stop=(k == final))
            if part[1] == KT:
                last.then_inc(unit_done, 1)

        u_hi3, u_lo3 = (a[:].rearrange("p (k t) -> p k t", t=T) for a in (a_hi, a_lo))
        y_hi3, y_lo3 = (a[:, 0:KT * L].rearrange("p (k t) -> p k t", t=L) for a in (a_hi, a_lo))
        h_hi3, h_lo3 = (a[:].rearrange("p (k t) -> p k t", t=L) for a in (h_hi, h_lo))

        def leave(eng, k):
            eng.drain().then_inc(S["left"], 1)
            eng.wait_ge(S["left"], 4 * k)

        def d3(ap, n):
            return ap.rearrange("p (a b) -> p a b", b=n)

        def rows4(ap):
            return ap.rearrange("p (r w) -> p r w", w=ROW + 2)[:, :, 0:ROW]

        def half_blocks(ap, level, d, which):
            w = 1 << level
            k = (d == 0) == (which == "new")
            return ap.rearrange("p (m two w) -> p m two w", two=2, w=w)[:, :, int(k)]

        def bc(ap2, n):
            return ap2.unsqueeze(2).broadcast_to([P, ap2.shape[1], n])

        def over(ap2, n):
            return ap2.unsqueeze(1).broadcast_to([P, n, ap2.shape[1]])

        block = ctx.enter_context(nc.Block())

        def tiles(eng, g, per, body, own=None):
            if g == 0:
                with eng.Fori(0, 2) as i:
                    if own:
                        own.begin(i, per)
                    for t in range(2):
                        body(i, t, True)
                if own:
                    own.end(2)
            else:
                for t in range(4, TS):
                    body(0, t, t + 1 < TS)

        def pairs(eng, head, per=0, own=None):
            head(0, 0)
            head(0, 1)
            with eng.Fori(1, HEADS // 2) as i:
                if own:
                    own.begin(i, per, 1)
                head(i, 0)
                head(i, 1)
            if own:
                own.end(HEADS // 2 - 1)

        @block.sync
        def _(sp):
            def load(n, r, wait):
                if wait is not None:
                    sp.wait_ge(lo_ready, wait)
                sp.dma_start(raw[r][:], stream[ds(n, 1) if not isinstance(n, int) else slice(n, n + 1)]
                             .rearrange("a p m -> p (a m)")).then_inc(raw_ready[r], 16)

            for n in range(RAW):
                load(n, n, None)
            for r in range(RAW):
                load(RAW + r, r, r + 1)
                sp.dma_start(d3(xr[:, r * 4 * T:(r + 1) * 4 * T], T),
                             x_dram[r * 512:(r + 1) * 512, :].rearrange("(k p) t -> p k t", p=P)).then_inc(S["ld_x"], 16)
            with sp.Fori(2, N_UNITS // RAW) as i:
                for r in range(RAW):
                    load(i * RAW + r, r, i * RAW + (r - RAW + 1))
            for n in range(N_UNITS // RAW * RAW, N_UNITS):
                load(n, n % RAW, n - RAW + 1)
            for q in range(4):
                sp.wait_ge(S["x_final"], 4 * (q + 1))
                sp.dma_start(out_dram[q * 512:(q + 1) * 512, :].rearrange("(k p) t -> p k t", p=P),
                             d3(x_res[:, q * 4 * L:(q + 1) * 4 * L], L)).then_inc(S["out_done"], 16)
            sp.wait_ge(S["out_done"], 64)
            sp.wait_ge(S["rel_out"], 32)

        @block.gpsimd
        def _(pool):
            own = Chain(pool, S["pool_own"])
            pool.dma_start(relb[0:BUCKETS, :], rel_dram).then_inc(S["ld_rel"], 16)
            pool.dma_start(onehot[0:BUCKETS + 1, :], bucket_dram).then_inc(S["ld_rel"], 16)
            pool.memset(relb[BUCKETS:BUCKETS + 1, :], -BIG).then_inc(S["rel_set"], 1)
            pool.dma_start(masks[:], const_dram[:, KEEP:N_CONST]).then_inc(S["ld_masks"], 16)
            pool.wait_ge(S["rel_set"], 1)
            pool.memset(EPS_C, EPS)
            pool.memset(QS_C, -0.5 * math.log(HG * 16))
            pool.memset(ONE_C, 1.0)
            pool.memset(ZERO_C, 0.0).then_inc(S["cols_set"], 1)
            own.add(pool.memset(xsq[:, T:2 * T], 0.0))
            pool.wait_ge(S["ld_x"], 64)
            with pool.Fori(0, KT) as i:
                own.begin(i, 2)
                x = xr[:, ds(i * T, T)]
                own.link(pool.tensor_tensor(xsq[:, 0:T], x, x, ALU.mult))
                own.link(pool.tensor_tensor(xsq[:, T:2 * T], xsq[:, T:2 * T], xsq[:, 0:T], ALU.add))
            own.end(KT)
            pool.tensor_copy(xsq[:, 0:T], xsq[:, T:2 * T]).then_inc(S["sq1"], 1)
            pool.wait_ge(S["rs1_ready"], 1)
            with pool.Fori(0, KT) as i:
                x = xr[:, ds(i * T, T)]
                pool.tensor_tensor(x, x, rs1[:], ALU.mult).then_inc(S["xr_ready"], 1)
            leave(pool, 1)
            leave(pool, 2)
            for j in range(3):
                last = pool.memset(g_pad[j][:], 0.0)
            last.then_inc(S["pads_set"], 1)

            with pool.Fori(0, HG) as i:
                pool.wait_ge(S["s_ready"], i * 6 + 1)
                pool.tensor_copy(g_w[:], wk_g[:, ds(i * 48, 48)]).then_inc(S["gw_ready"], 1)
                pool.wait_ge(S["l_ready"], i + 1)
                for level in range(LEVELS):
                    if level >= 2:
                        pool.wait_ge(S["x_mm"], i * (2 * LEVELS) + 2 * (level - 1))
                    if level == 2:
                        pool.wait_ge(S["first_ut"], i + 1)
                    for d in range(2):
                        m = pool.tensor_tensor(d3(g_M[level % 2][:, d * 512:d * 512 + 512], P),
                                               d3(g_L[:, d * 512:d * 512 + 512], P),
                                               over(K("level", d * LEVELS + level), 4), ALU.mult)
                    m.then_inc(S["m_ready"], 1)

            leave(pool, 3)
            pool.memset(s_pad[:], 0.0).then_inc(S["pads_set"], 1)
            for g in range(2):
                def columns_of(i, t, more):
                    pool.wait_ge(S["h_ready"], i * 2 + (t + 1))
                    pool.tensor_copy(s_w[:], wk_s[:, ds(i * 160 + t * 80, 80)]).then_inc(S["sw_ready"], 1)
                tiles(pool, g, 0, columns_of)
            leave(pool, 4)
            pool.wait_ge(S["rel_out"], 16)
            pool.dma_start(d3(turned[:], L), bass.AP(scratch[0].tensor, 0, [[1, P], [DIST, 2 * HEADS], [1, L]])
                           ).then_inc(S["turned_ready"], 16)
            for e in range(1 + 2 * LAYERS):
                if e == 1:
                    continue
                if e:
                    pool.wait_ge(S["ss_mm"], e)
                own.add(pool.memset(n_acc[:], 0.0))
                src, ready, at = (mo, S["mo_ready"], 0) if e == 0 else (x_res, S["sx_upd"], (e - 1) * KT)
                with pool.Fori(0, KT) as i:
                    own.begin(i, 2)
                    pool.wait_ge(ready, i + (at + 1))
                    tile = src[:, ds(i * L, L)]
                    own.link(pool.tensor_tensor(n_sq[:], tile, tile, ALU.mult))
                    own.link(pool.tensor_tensor(n_acc[:], n_acc[:], n_sq[:], ALU.add))
                own.end(KT)
                pool.tensor_copy(n_sq[:], n_acc[:]).then_inc(S["acc_ready"], 1)
                if e and e % 2 == 0:
                    l = e // 2 - 1
                    for q in range(FQ):
                        with pool.Fori(0, KT // 4) as i:
                            for j in range(4):
                                at = l * FQ * KT + q * KT + j + 1
                                pool.wait_ge(S["relu_ready"], i * 4 + at)
                                pool.wait_ge(S["mlp_ready"], i * 4 + at)
                                t = hbuf[:, (j % 2) * L:(j % 2) * L + L]
                                s = hbuf[:, (2 + j % 2) * L:(3 + j % 2) * L]
                                pool.tensor_tensor(s, t, t, ALU.mult).then_inc(S["sq_relu"], 1)

        @block.tensor
        def _(pe):
            mm = pe.matmul

            def each(bank, pairs, w=P, at=0):
                for n, (lhs, rhs) in enumerate(pairs):
                    last = mm(psum[bank][:, at + n * w:at + (n + 1) * w], lhs, rhs, start=True, stop=True)
                return last

            def turn(bank, tiles, at=0):
                for n, t in enumerate(tiles):
                    last = pe.transpose(psum[bank][:, at + n * P:at + (n + 1) * P], t, IDENT)
                return last

            def blocks(buf, d, n=4):
                return [buf[:, (d * n + c) * P:(d * n + c + 1) * P] for c in range(n)]

            pe.wait_ge(S["ld_par"], 32)
            pe.wait_ge(S["ld_rel"], 32)
            pe.wait_ge(S["rel_set"], 1)
            mm(psum[5][0:16, 0:DIST], relb[0:BUCKETS + 1, :], onehot[0:BUCKETS + 1, :], start=True, stop=True).then_inc(S["rel_mm"], 1)

            pe.wait_ge(S["c_ready"], 1)

            def modulation(i):
                for q in range(4):
                    u = Unit(q, i)
                    for w, ready in ((w_hi, hi_ready), (w_lo, lo_ready)):
                        pe.wait_ge(ready, u.n + 1)
                        for k in range(4):
                            m = mm(psum[2][0:4, :], c4[:, (q * 4 + k) * 4:(q * 4 + k) * 4 + 4], w[u.slot][:, k * 512:(k + 1) * 512],
                                   start=(q + k == 0 and w is w_hi), stop=(q * 4 + k == 15 and w is w_lo))
                    m.then_inc(unit_done, 1)
                pe.wait_ge(S["mrow_ready"], i + 1)
                for j in range(4):
                    m = mm(psum[3][:, ds(i * 8 + j * 2, 2)], mrow[0:4, j * P:(j + 1) * P], K("sel", 0, 2)[0:4, :],
                           start=True, stop=True)
                m.then_inc(S["ada_cols"], 1)

            with pe.Fori(0, EARLY) as i:
                modulation(i)
            pe.wait_ge(S["sq1"], 1)
            mm(psum[4][:], ONES, xsq[:, 0:T], start=True, stop=True).then_inc(S["ss1"], 1)
            with pe.Fori(EARLY, 12) as i:
                modulation(i)

            unit_mm(pe, Unit(U_SMALL), u_hi3, u_lo3, T, comes=(S["u_ready"], {k: k + 1 for k in range(KT)}))
            leave(pe, 1)
            pe.wait_ge(S["sm_beta"], 1)
            turn(2, [sm_e[:, c * P:(c + 1) * P] for c in range(C)]).then_inc(S["sm_turned"], 1)
            pe.wait_ge(S["tm_ready"], 1)
            pe.wait_ge(S["ld_masks"], 16)
            log = d3(tm[:], P)[:, :, 0:48]
            for d in range(2):
                mm(d3(psum[3][:, d * 192:d * 192 + 192], 48), K("tri", d), log, start=True, stop=True)
            mm(d3(psum[4][:, 0:192], 48), ONES, log, start=True, stop=True).then_inc(S["sm_sums"], 1)
            leave(pe, 2)

            def head(i, more):
                def ahead(j, k0, k1):
                    if more:
                        unit_mm(pe, Unit(U_GDN + 4 + j, i), u_hi3, u_lo3, T if j in (1, 2) else L, part=(k0, k1))
                pe.wait_ge(S["gw_ready"], i + 1)
                for d in range(2):
                    m = each(6 + d, [(g_w[:, d * 4 + c:d * 4 + c + 1].broadcast_to([P, P]), K("tri", d)) for c in range(C)])
                m.then_inc(S["g_rows"], 1)
                pe.wait_ge(S["sq_ready"], i + 1)
                mm(psum[2][:], ONES, g_X[:, 0:T], start=True, stop=True)
                mm(psum[3][:, 0:L], ONES, g_X[:, T:T + L], start=True, stop=True).then_inc(S["g_ss"], 1)
                ahead(0, 0, KT)
                pe.wait_ge(S["kn_ready"], i + 1)
                kn = [g_k[:, c * P:(c + 1) * P] for c in range(C)]
                each(4, [(k, k) for k in kn]).then_inc(S["gram"], 1)
                each(5, [(kn[c], g_q[:, c * P:(c + 1) * P]) for c in range(2)]).then_inc(S["gram"], 1)
                ahead(1, 0, 5)
                pe.wait_ge(S["m_ready"], i * LEVELS + 1)
                for d in range(2):
                    m = turn(2 + d, blocks(g_M[0], d))
                    m.then_inc(S["x_mm"], 1)
                ahead(1, 5, 9)
                for level in range(1, LEVELS):
                    pe.wait_ge(S["m_ready"], i * LEVELS + (level + 1))
                    for d in range(2):
                        if level == 1:
                            pe.wait_ge(S["first_ut"], i + 1)
                        else:
                            pe.wait_ge(S["ut_ready"], i * 12 + (2 * (level - 2) + d + 1))
                        each(4 + d, zip(blocks(g_M[level % 2], d), blocks(g_U, d))).then_inc(S["x_mm"], 1)
                    if level < LEVELS - 1:
                        ahead(*FILL[level])
                    for d in range(2):
                        pe.wait_ge(S["xp_ready"], i * 12 + (2 * (level - 1) + d + 1))
                        m = each(6 + d, [(t, half_blocks(x, level, d, "new")) for t, x in zip(blocks(g_T, d), blocks(g_X, d))], w=64)
                        if level < LEVELS - 1:
                            m = each(2 + d, [(x, half_blocks(t, level, d, "old"))
                                             for t, x in zip(blocks(g_T, d), blocks(g_X, d))], w=64)
                        m.then_inc(S["uu_mm"], 1)
                turn(2, kn).then_inc(S["nw_mm"], 1)
                turn(3, [g_v[:, c * P:(c + 1) * P] for c in range(C)]).then_inc(S["nw_mm"], 1)
                pe.wait_ge(S["tok_used"], i * 2 + 1)
                for d in range(2):
                    pe.wait_ge(S["ut_ready"], i * 12 + (10 + d + 1))
                    each(4 + d, zip(blocks(g_kb, d), blocks(g_U, d))).then_inc(S["nw_mm"], 1)
                pe.wait_ge(S["aq_ready"], i + 1)
                pe.wait_ge(S["tok_used"], i * 2 + 2)
                ahead(3, 0, 2)
                for step in range(4):
                    for d in range(2):
                        c = ORDER[d][step]
                        b = d * 4 + c
                        if step == 0:
                            pe.wait_ge(S["nw_ready"], i * 2 + (d + 1))
                        else:
                            pe.wait_ge(S["s_ready"], i * 6 + (2 * (step - 1) + d + 2))
                        vn = psum[6 + d][:, 0:P]
                        m = mm(vn, g_U[:, b * P:(b + 1) * P], g_vb[:, b * P:(b + 1) * P], start=True, stop=(step == 0))
                        if step:
                            m = mm(vn, g_T[:, b * P:(b + 1) * P], g_S[:, d * P:(d + 1) * P], start=False, stop=True)
                        m.then_inc(S["vn_mm"], 1)
                        if step >= 2:
                            a = d * 2 + c
                            mm(psum[4][:, c * P:(c + 1) * P], g_S[:, d * P:(d + 1) * P], g_qd[:, a * P:(a + 1) * P],
                               start=(step == 2 and d == 0), stop=False, skip_group_check=True)
                    ahead(3, 2 + 3 * step, 5 + 3 * step)
                    for d in range(2):
                        c = ORDER[d][step]
                        b = d * 4 + c
                        pe.wait_ge(S["vn_ready"], i * 8 + (2 * step + d + 1))
                        v = g_vn[:, d * P:(d + 1) * P]
                        if step < 3:
                            mm(psum[2 + d][:, 0:P], g_ke[:, b * P:(b + 1) * P], v, start=True, stop=True).then_inc(S["s_mm"], 1)
                        if step >= 2:
                            a = d * 2 + c
                            m = mm(psum[4][:, c * P:(c + 1) * P], v, g_A[:, a * P:(a + 1) * P],
                                   start=False, stop=(step == 3), skip_group_check=True)
                m.then_inc(S["o_mm"], 1)
                pe.wait_ge(S["osq_ready"], i + 1)
                mm(psum[5][:, 0:L], ONES, g_X[:, 0:L], start=True, stop=True).then_inc(S["oss"], 1)
                ahead(3, 14, KT)

            for j in range(4):
                unit_mm(pe, Unit(U_GDN + j), u_hi3, u_lo3, T if j in (1, 2) else L)
            with pe.Fori(0, HG - 1) as i:
                head(i, True)
            head(HG - 1, False)

            leave(pe, 3)
            for j in range(4):
                unit_mm(pe, Unit(U_BC + j), u_hi3, u_lo3, T if j < 2 else L)
            unit_mm(pe, Unit(U_SSD), u_hi3, u_lo3, T)
            unit_mm(pe, Unit(U_SSD + 1), u_hi3, u_lo3, L)
            pe.wait_ge(S["bc_ready"], 4)
            for g in range(2):
                m = turn(2 + g, [s_bt[:, g * T + c * P:g * T + (c + 1) * P] for c in range(C)])
            for g in range(2):
                m = each(4, [(s_bt[:, g * T + c * P:g * T + (c + 1) * P], s_ct[:, g * L + c * P:g * L + (c + 1) * P])
                             for c in range(2)], at=g * 2 * P)
            m.then_inc(S["b_turned"], 1)
            for g in range(2):
                def tile(i, t, more):
                    nxt = Unit(U_SSD + 2 * t + 2, i)
                    pe.wait_ge(S["sw_ready"], i * 2 + (t + 1))
                    pe.wait_ge(S["bc_tok"], 1)
                    for d in range(2):
                        m = each(3 + d, [(s_w[:, d * 8 + e:d * 8 + e + 1].broadcast_to([P, P]), K("tri", d))
                                         for e in range(4)])
                    m.then_inc(S["s_rows"], 1)
                    pe.wait_ge(S["sx_ready"], i * 2 + (t + 1))
                    turn(2, [s_x[t % 2][:, c * P:(c + 1) * P] for c in range(C)]).then_inc(S["s_tok"], 1)
                    if more:
                        unit_mm(pe, nxt, u_hi3, u_lo3, T)
                    pe.wait_ge(S["s_de_ready"], i * 2 + (t + 1))
                    for d in range(2):
                        m = each(5 + d, [(s_btok[:, g * T + c * P:g * T + (c + 1) * P],
                                          s_de[:, (d * 4 + c) * P:(d * 4 + c + 1) * P]) for c in ORDER[d][0:3]])
                    m.then_inc(S["st_mm"], 1)
                    if more:
                        unit_mm(pe, nxt.ahead(1), u_hi3, u_lo3, L)
                    pe.wait_ge(S["s_mc_ready"], i * 2 + (t + 1))
                    pe.wait_ge(S["h_ready"], i * 2 + (t + 2))
                    for e in range(2):
                        for c in range(2):
                            o = psum[7][e * 64:e * 64 + 64, c * P:(c + 1) * P]
                            for d in range(2):
                                b = (d * 2 + c) * 2 + e
                                x = s_dt[:, (d * 2 + c) * P + e * 64:(d * 2 + c) * P + e * 64 + 64]
                                mm(o, x, s_M[:, b * P:(b + 1) * P], start=(c == 0 and d == 0), stop=False, skip_group_check=True)
                                s = (d * 3 + ORDER[d].index(c) - 1) * P + e * 64
                                m = mm(o, s_H[:, s:s + 64], s_C[:, b * P:(b + 1) * P], start=False, stop=(d == 1),
                                       skip_group_check=True)
                    m.then_inc(S["y_mm"], 1)
                tiles(pe, g, 0, tile)
                pe.wait_ge(S["grp_sq"], g + 1)
                for k in range(4):
                    m = mm(psum[7][:, 0:L], ONES, s_M[:, k * L:(k + 1) * L], start=(k == 0), stop=(k == 3))
                m.then_inc(S["grp_ss"], 1)
            leave(pe, 4)

            quarters = (S["y_ready"], {4 * q: q + 1 for q in range(4)})
            for j in range(4):
                unit_mm(pe, Unit(U_WOUT + j), y_hi3, y_lo3, L, None if j else quarters)
            pe.wait_ge(S["turned_ready"], 16)
            for k in range(8):
                if k >= 6:
                    pe.wait_ge(S["flip_read"], k - 5)
                mm(psum[2 + k % 6][:], K("flip"), turned[:, k * 512:(k + 1) * 512], start=True, stop=True).then_inc(S["flip_mm"], 1)
            with pe.Fori(1, KT // 4) as i:
                for j in range(4):
                    unit_mm(pe, Unit(U_WOUT + j, i), y_hi3, y_lo3, L)

            def norm_sums(e):
                if e == 1:
                    for k in range(KT):
                        pe.wait_ge(S["x_sq"], k + 1)
                        mm(psum[2][:, 0:L], ONES, (n_sq, n_acc)[k % 2][:], start=(k == 0), stop=(k == KT - 1)
                           ).then_inc(S["x_sq_used" if k < KT - 1 else "ss_mm"], 1)
                    return
                pe.wait_ge(S["acc_ready"], e + 1 - (e > 1))
                mm(psum[2][:, 0:L], ONES, n_sq[:], start=True, stop=True).then_inc(S["ss_mm"], 1)

            norm_sums(0)
            for l in range(LAYERS):
                base = U_LAYER + l * N_LAYER
                norm_sums(1 + 2 * l)
                normed = (S["h_ready2"], {2 * k: 2 * l * 8 + k + 1 for k in range(8)})
                def at(i, j, n=1, k=1):
                    return i * (2 * n) + ((l * HEADS + j) * n + k)

                def turn_p(i, j):
                    pe.wait_ge(S["p_ready"], at(i, j))
                    turn(6, [b_s[:, L:L + P], b_s[:, 0:P], b_s[:, P:L]]).then_inc(S["pt_mm"], 1)

                def p_times_v(i, j):
                    pe.wait_ge(S["pt_ready"], at(i, j))
                    pe.wait_ge(S["vt_ready"], at(i, j))
                    mm(psum[7][:, 0:L], b_vt[:, 0:P], b_pt[:, 0:L], start=True, stop=False, skip_group_check=True)
                    mm(psum[7][:, P:L], b_vt[:, P:L], b_pt[:, L:L + P], start=False, stop=True,
                       skip_group_check=True).then_inc(S["av_mm"], 1)

                def squares_sum(i, j):
                    pe.wait_ge(S["av_sq"], at(i, j))
                    mm(psum[7][:, L:2 * L], ONES, b_os[:], start=True, stop=True).then_inc(S["av_ss"], 1)

                def head(i, j):
                    last = None if isinstance(i, int) and i + j == 0 else (i, j - 1)
                    u = Unit(base + 6 * j, i, 3)
                    unit_mm(pe, u, h_hi3, h_lo3, L, normed if last is None else None)
                    if last:
                        turn_p(*last)
                    unit_mm(pe, u.ahead(1), h_hi3, h_lo3, L)
                    if last:
                        p_times_v(*last)
                    unit_mm(pe, u.ahead(2), h_hi3, h_lo3, L)
                    pe.wait_ge(S["qk_sq"], at(i, j, 2, 2))
                    mm(psum[2][:], K("blk"), b_qs[:], start=True, stop=True).then_inc(S["qk_ss"], 1)
                    if last:
                        squares_sum(*last)
                    unit_mm(pe, u.ahead(3), h_hi3, h_lo3, L)
                    pe.wait_ge(S["qk_ready"], at(i, j))
                    for m_ in range(2):
                        rows = slice(m_ * DK, (m_ + 1) * DK)
                        mm(psum[3 + m_][:, 0:L], b_qk[rows, P:L], b_qk[rows, L:2 * L], start=True, stop=True)
                        m = mm(psum[3 + m_][:, L:L + P], b_qk[rows, 0:P], b_qk[rows, L:L + P], start=True, stop=True)
                    m.then_inc(S["score_mm"], 1)
                    pe.wait_ge(S["v_ready"], at(i, j))
                    turn(5, [b_v[:, 0:P], b_v[:, P:L]]).then_inc(S["vt_mm"], 1)
                    unit_mm(pe, u.ahead(4), h_hi3, h_lo3, L)
                    unit_mm(pe, u.ahead(5), h_hi3, h_lo3, L)
                pairs(pe, head)
                for step in (turn_p, p_times_v, squares_sum):
                    step(HEADS // 2 - 1, 1)
                order = [k for k in range(KT) if k != HEADS - 1] + [HEADS - 1]
                mixed = (S["yt_ready"], {0: (l + 1) * 2 * HEADS - 1, HEADS - 1: (l + 1) * 2 * HEADS})
                with pe.Fori(0, KT // 4) as i:
                    for j in range(4):
                        unit_mm(pe, Unit(base + N_IN2 + j, i), y_hi3, y_lo3, L, None if j else mixed, order)
                norm_sums(2 + 2 * l)
                normed = (S["h_ready2"], {2 * k: (2 * l + 1) * 8 + k + 1 for k in range(8)})
                c = base + N_IN2 + KT
                for kind, q in MLP_ORDER:
                    if kind == "up":
                        hi, lo = h_hi3, h_lo3
                    else:
                        pe.wait_ge(S["mlp_ready"], (l * FQ + q + 1) * KT + 2)
                        hi, lo = (a[:, (q % 2) * KT * L:(q % 2 + 1) * KT * L].rearrange("p (k t) -> p k t", t=L)
                                  for a in (a_hi, a_lo))
                    with pe.Fori(0, KT // 4) as i:
                        for j in range(4):
                            unit_mm(pe, Unit(c + j, i), hi, lo, L, normed if (kind, q, j) == ("up", 0, 0) else None)
                    c += KT

        @block.scalar
        def _(act):
            own = Chain(act, S["act_own"])
            f = act.activation

            def root(out, in_, tmp, scale, last, bias=None):
                own.link(f(tmp, in_, ACT.Ln, bias=EPS_C, scale=scale))
                f(out, tmp, ACT.Exp, bias=ZERO_C if bias is None else bias, scale=-0.5).then_inc(S[last], 1)

            act.dma_start(keep[:], const_dram[:, 0:KEEP]).then_inc(S["ld_par"], 16)
            act.dma_start(pars[:, 0:N_PAR], par_dram).then_inc(S["ld_par"], 16)
            act.wait_ge(S["ld_par"], 32)
            act.wait_ge(S["cols_set"], 1)
            own.link(f(cs[:], par("c", 0, 2 * KT), ACT.Silu))
            act.copy(d3(c4[:], 4)[:, :, 0:2], d3(cs[:], 2)).then_inc(S["c_silu"], 1)
            split_act_halves(act, Unit(0))
            split_act_halves(act, Unit(1))
            act.preload_act_table_set(LOG_EXP)
            act.wait_ge(S["rel_copy"], 1)
            act.dma_start(scratch[0], by_dist[0:16, :]).then_inc(S["rel_out"], 16)

            def modulation(i):
                for q in range(4):
                    u = Unit(q, i)
                    act.wait_ge(unit_done, u.n + 1)
                    if q == 3:
                        act.copy(mrow[0:4, :], psum[2][0:4, :]).then_inc(S["mrow_ready"], 1)
                    split_act_halves(act, u.ahead(2))

            with act.Fori(0, EARLY) as i:
                modulation(i)
            act.wait_ge(S["ss1"], 1)
            root(rs1[:], psum[4][:], ln1[:], 1.0 / D, "rs1_ready")
            with act.Fori(EARLY, 12) as i:
                modulation(i)
            for k in range(KT):
                act.wait_ge(S["u_f32"], k + 1)
                act.copy(a_hi[:, k * T:(k + 1) * T], xr[:, k * T:(k + 1) * T]).then_inc(S["u_hi"], 1)
            leave(act, 1)
            act.wait_ge(S["sm_lin"], 1)
            own.link(f(sm_e[:], sm[:], ACT.Abs))
            own.link(f(sm_e[:], sm_e[:], ACT.Exp, scale=-1.0))
            f(gmul[:, 0:1], par("a_log"), ACT.Exp)
            f(sm_e[:], sm_e[:], ACT.Ln, bias=ONE_C).then_inc(S["sm_soft"], 1)
            split_act(act, Unit(U_SMALL + 2))
            act.wait_ge(S["sm_mul"], 1)
            f(sm_e[64:96, :], sm[64:96, :], ACT.Exp, scale=-1.0).then_inc(S["sm_beta"], 1)
            act.wait_ge(S["sm_turned"], 1)
            act.copy(tm[:], psum[2][:]).then_inc(S["tm_ready"], 1)
            act.wait_ge(S["sm_cum"], 1)
            f(gexp[:], gcum[:], ACT.Exp)
            f(gdec[:], gtot[:], ACT.Exp)
            f(gend[:], gend[:], ACT.Exp).then_inc(S["sm_exp"], 1)
            leave(act, 2)

            act.wait_ge(S["pads_set"], 1)
            act.wait_ge(S["rel_out"], 16)
            def padded(u, j):
                v = u.ahead(j)
                act.wait_ge(unit_done, v.n + 1)
                bank = psum[v.bank]
                m = act.copy(rows4(g_pad[j][:, 2:PADW]), d3(bank[:, 0:L], ROW))
                if j:
                    m = act.copy(g_pad[j][:, PADW:PADW + L], bank[:, L:T])
                m.then_inc(S["pad_ready"], 1)
                split_act(act, v.ahead(2))

            def silu(i, k, j):
                out = (g_q, g_k, g_v)[j]
                act.wait_ge(S["conv_done"], i * 3 + (k * 3 + j + 1))
                m = f(d3(out[:, 0:L], ROW), rows4(g_acc[j][:, 0:264]), ACT.Silu)
                if j:
                    m = f(out[:, L:T], g_acc[j][:, 264:520], ACT.Silu)
                return m

            def head(i, more):
                u = Unit(U_GDN, i)
                f(g_X[:, 0:T], g_k[:], ACT.Square)
                f(g_X[:, T:T + L], g_q[:], ACT.Square).then_inc(S["sq_ready"], 1)
                z = u.ahead(3)
                gate = x_res[:, ds(i * L + HG * L, L)]
                act.wait_ge(unit_done, z.n + 1)
                act.copy(gate, psum[z.bank][:, 0:L])
                act.wait_ge(S["g_ss"], i + 1)
                act.wait_ge(S["head_done"], i + 1)
                own.add(f(g_M[0][:, T:T + L], psum[3][:, 0:L], ACT.Ln, bias=EPS_C))
                own.link(f(g_M[0][:, 0:T], psum[2][:], ACT.Ln, bias=EPS_C))
                f(g_M[0][:, T:T + L], g_M[0][:, T:T + L], ACT.Exp, bias=QS_C, scale=-0.5)
                f(g_M[0][:, 0:T], g_M[0][:, 0:T], ACT.Exp, scale=-0.5).then_inc(S["gr_ready"], 1)
                split_act(act, z.ahead(2))
                act.wait_ge(S["dpre"], i + 1)
                f(g_L[:], g_L[:], ACT.Exp, scale=-1.0)
                f(g_A[:], g_A[:], ACT.Exp)
                f(g_qd[:, 0:L], psum[6][:, 0:L], ACT.Exp)
                f(g_qd[:, L:2 * L], psum[7][:, 0:L], ACT.Exp).then_inc(S["dexp"], 1)
                if more:
                    padded(u.ahead(4), 0)
                for level in range(1, LEVELS):
                    for d in range(2):
                        act.wait_ge(S["uu_mm"], i * 12 + (2 * (level - 1) + d + 1))
                        half = slice(d * 512, d * 512 + 512)
                        m = act.copy(half_blocks(g_U[:, half], level, d, "new"), d3(psum[6 + d][:, 0:L], 1 << level))
                        if level < LEVELS - 1:
                            m = act.copy(half_blocks(g_T[:, half], level, d, "old"), d3(psum[2 + d][:, 0:L], 1 << level))
                        m.then_inc(S["ut_ready"], 1)
                    if more and level in (3, 5):
                        padded(u.ahead(4), 1 if level == 3 else 2)
                for d in range(2):
                    act.wait_ge(S["nw_mm"], i * 4 + (3 + d))
                    act.mul(g_T[:, d * 512:d * 512 + 512], psum[4 + d][:], -1.0).then_inc(S["nw_ready"], 1)
                act.wait_ge(S["aq_ready"], i + 1)
                for step in range(4):
                    for d in range(2):
                        act.wait_ge(S["vn_mm"], i * 8 + (2 * step + d + 1))
                        act.copy(g_vn[:, d * P:(d + 1) * P], psum[6 + d][:, 0:P]).then_inc(S["vn_ready"], 1)
                    if more and step < 3:
                        silu(i, 1, step)
                    if step == 2:
                        f(gate, gate, ACT.Silu)
                act.wait_ge(S["o_mm"], i + 1)
                f(g_X[:, 0:L], psum[4][:, 0:L], ACT.Square).then_inc(S["osq_ready"], 1)
                act.preload_act_table_set(LOG_EXP)
                act.wait_ge(S["oss"], i + 1)
                root(g_M[0][:, L:2 * L], psum[5][:, 0:L], g_M[0][:, 0:L], 1.0 / P, "o_rs")

            for j in range(3):
                padded(Unit(U_GDN), j)
            for j in range(3):
                m = silu(0, 0, j)
            own.link(m)
            act.preload_act_table_set(LOG_EXP)
            with act.Fori(0, HG - 1) as i:
                own.begin(i, 3)
                head(i, True)
            own.end(HG - 1)
            head(HG - 1, False)

            leave(act, 3)
            act.wait_ge(S["pads_set"], 2)
            for j in range(4):
                u = Unit(U_BC + j)
                act.wait_ge(unit_done, u.n + 1)
                bank = psum[u.bank]
                m = act.copy(rows4(s_pad[:, 2:PADW]), d3(bank[:, 0:L], ROW))
                if j < 2:
                    m = act.copy(s_pad[:, PADW:PADW + L], bank[:, L:T])
                m.then_inc(S["bc_pad"], 1)
                split_act(act, u.ahead(2))
                act.wait_ge(S["bc_conv"], j + 1)
                out = s_bt[:, j * T:(j + 1) * T] if j < 2 else s_ct[:, (j - 2) * L:(j - 1) * L]
                m = f(d3(out[:, 0:L], ROW), rows4(s_acc[:, 0:264]), ACT.Silu, bias=par("bias_ssd", 8 + j))
                if j < 2:
                    m = f(out[:, L:T], s_acc[:, 264:520], ACT.Silu, bias=par("bias_ssd", 8 + j))
                m.then_inc(S["bc_ready"], 1)

            def tile_in(i, t):
                u = Unit(U_SSD + 2 * t, i)
                act.wait_ge(unit_done, u.n + 1)
                bank = psum[u.bank]
                act.copy(rows4(s_pad[:, 2:PADW]), d3(bank[:, 0:L], ROW))
                act.copy(s_pad[:, PADW:PADW + L], bank[:, L:T]).then_inc(S["sx_pad"], 1)
                split_act(act, u.ahead(2))
                act.wait_ge(S["sx_conv"], i * 2 + (t + 1))
                b = par("bias_ssd", i * 2 + t)
                out = s_x[t % 2]
                f(d3(out[:, 0:L], ROW), rows4(s_acc[:, 0:264]), ACT.Silu, bias=b)
                f(out[:, L:T], s_acc[:, 264:520], ACT.Silu, bias=b).then_inc(S["sx_ready"], 1)
                u = u.ahead(1)
                act.wait_ge(unit_done, u.n + 1)
                f(x_res[:, ds(i * (2 * L) + t * L, L)], psum[u.bank][:, 0:L], ACT.Silu)
                split_act(act, u.ahead(2))
                act.preload_act_table_set(LOG_EXP)
            tile_in(0, 0)
            act.wait_ge(S["b_turned"], 1)
            act.copy(s_btok[:, 0:T], psum[2][:])
            act.copy(s_btok[:, T:2 * T], psum[3][:])
            act.copy(s_cb[:], psum[4][:]).then_inc(S["bc_tok"], 1)
            for g in range(2):
                def tile(i, t, more):
                    act.wait_ge(S["s_pre"], i * 2 + (t + 1))
                    f(s_M[:], s_M[:], ACT.Exp)
                    f(s_C[:, 0:T], psum[3][:], ACT.Exp)
                    f(s_C[:, T:2 * T], psum[4][:], ACT.Exp).then_inc(S["s_exp"], 1)
                    if more:
                        tile_in(i, t + 1)
                tiles(act, g, 0, tile)
                act.wait_ge(S["tile_done"], 4 * (g + 1) + 1)
                f(s_M[:], x_res[:, g * 4 * L:(g + 1) * 4 * L], ACT.Square).then_inc(S["grp_sq"], 1)
                act.wait_ge(S["grp_ss"], g + 1)
                root(s_y[:], psum[7][:, 0:L], s_r[:], 1.0 / 512, "grp_rs")
            leave(act, 4)

            for q in range(4):
                act.copy(a_hi[:, q * 1024:(q + 1) * 1024], x_res[:, q * 1024:(q + 1) * 1024]).then_inc(S["y_hi"], 1)
            act.wait_ge(S["y_ready"], 4)
            act.dma_start(d3(x_res[:], L), x_dram[:, 0:L].rearrange("(k p) t -> p k t", p=P)).then_inc(S["x_loaded"], 16)

            def projected4(i):
                for j in range(4):
                    u = Unit(U_WOUT + j, i)
                    act.wait_ge(unit_done, u.n + 1)
                    act.copy(mo[:, ds(i * (4 * L) + j * L, L)], psum[u.bank][:, 0:L]).then_inc(S["mo_ready"], 1)
                    split_act(act, u.ahead(2))
            projected4(0)
            for k in range(8):
                act.wait_ge(S["flip_mm"], k + 1)
                act.copy(bias[:, k * 512:(k + 1) * 512], psum[2 + k % 6][:]).then_inc(S["flip_read"], 1)
            act.wait_ge(S["flip_read"], 8)
            act.dma_start(scratch[1], bias[:]).then_inc(S["rel_out"], 16)
            with act.Fori(1, KT // 4) as i:
                projected4(i)

            def norm_root(e):
                if e == 1:
                    for k in range(KT):
                        act.wait_ge(S["sx_upd"], k + 1)
                        if k >= 2:
                            act.wait_ge(S["x_sq_used"], k - 1)
                        f((n_sq, n_acc)[k % 2][:], x_res[:, k * L:(k + 1) * L], ACT.Square).then_inc(S["x_sq"], 1)
                act.wait_ge(S["ss_mm"], e + 1)
                root(n_rs[:], psum[2][:, 0:L], n_ln[:], 1.0 / D, "rs_ready")

            def norm_hi(e):
                for g in range(8):
                    act.wait_ge(S["h_f32"], e * 8 + g + 1)
                    act.copy(h_hi[:, g * T:(g + 1) * T], hbuf[:, (g % 2) * T:(g % 2) * T + T]).then_inc(S["h_hi_ready"], 1)

            norm_root(0)
            act.wait_ge(S["lam_d"], 1)
            f(small[:, 20:24], small[:, 16:20], ACT.Exp).then_inc(S["lam_e"], 1)
            for l in range(LAYERS):
                base = U_LAYER + l * N_LAYER
                act.preload_act_table_set(LOG_EXP)
                norm_root(1 + 2 * l)
                norm_hi(2 * l)
                if l:
                    act.dma_start(bias[:], scratch[1]).then_inc(S["bias_ready"], 16)
                def at(i, j):
                    return i * 2 + (l * HEADS + j + 1)

                def pt_copy(i, j):
                    act.wait_ge(S["pt_mm"], at(i, j))
                    act.copy(b_pt[:], psum[6][:, 0:3 * P]).then_inc(S["pt_ready"], 1)

                def av_square(i, j):
                    act.wait_ge(S["av_mm"], at(i, j))
                    f(b_os[:], psum[7][:, 0:L], ACT.Square).then_inc(S["av_sq"], 1)

                def av_root(i, j):
                    act.wait_ge(S["av_ss"], at(i, j))
                    root(b_or[:], psum[7][:, L:2 * L], b_ol[:], 1.0 / P, "av_rs")

                def av_hi(i, j):
                    act.wait_ge(S["attn_f32"], at(i, j))
                    act.copy(a_hi[:, ds(i * (2 * L) + j * L, L)], b_o[:]).then_inc(S["attn_hi"], 1)

                def head(i, j):
                    last = None if isinstance(i, int) and i + j == 0 else (i, j - 1)
                    u = Unit(base + 6 * j, i, 3)

                    def projected(m):
                        act.wait_ge(unit_done, u.ahead(m).n + 1)
                        return psum[u.ahead(m).bank][:, 0:L]
                    for m in range(2):
                        act.copy(b_qk[:, m * L:(m + 1) * L], projected(m))
                        f(b_qs[:, m * L:(m + 1) * L], psum[u.ahead(m).bank][:, 0:L], ACT.Square).then_inc(S["qk_sq"], 1)
                        split_act(act, u.ahead(m + 2))
                        if last:
                            (pt_copy, av_square)[m](*last)
                    act.copy(b_v[:], projected(2)).then_inc(S["v_ready"], 1)
                    split_act(act, u.ahead(4))
                    act.wait_ge(S["qk_ss"], at(i, j))
                    root(b_rs[:], psum[2][:], b_rs[:], 1.0 / DK, "rs_qk")
                    if last:
                        av_root(*last)
                    act.copy(b_gb[:], projected(3))
                    split_act(act, u.ahead(5))
                    if last:
                        av_hi(*last)
                    act.wait_ge(S["vt_mm"], at(i, j))
                    act.copy(b_vt[:], psum[5][:, 0:L]).then_inc(S["vt_ready"], 1)
                    act.copy(b_gc[:], projected(4))
                    split_act(act, u.ahead(6))
                    act.wait_ge(S["sc_ready"], at(i, j))
                    for m, (a, b) in enumerate(((0, L), (3 * P, 3 * P + L), (L, 3 * P), (3 * P + L, 6 * P))):
                        e = f(b_s[:, a:b], b_s[:, a:b], ACT.Exp, bias=b_st[:, m:m + 1], accum_out=b_st[:, 4 + m:5 + m])
                    e.then_inc(S["p_exp"], 1)
                    act.copy(b_ci[:], projected(5)).then_inc(S["gates_ready"], 1)
                    split_act(act, u.ahead(7))
                    tile = i * (2 * L) + j * L
                    act.wait_ge(S["conv_f32"], at(i, j))
                    act.copy(a_hi[:, ds(tile + HEADS * L, L)], b_co[:]).then_inc(S["conv_hi"], 1)
                pairs(act, head, 2 * 2, own)
                for step in (pt_copy, av_square, av_root, av_hi):
                    step(HEADS // 2 - 1, 1)
                with act.Fori(0, KT // 4) as i:
                    for j in range(4):
                        split_act(act, Unit(base + N_IN2 + j + 2, i))
                norm_root(2 + 2 * l)
                norm_hi(2 * l + 1)
                act.wait_ge(S["rel_out"], 32)
                c = base + N_IN2 + KT
                for kind, q in MLP_ORDER:
                    def turn_(i, j):
                        u = Unit(c + j, i)
                        if kind == "up":
                            at = (l * FQ + q) * KT + j + 1
                            act.wait_ge(unit_done, u.n + 1)
                            f(hbuf[:, (j % 2) * L:(j % 2) * L + L], psum[u.bank][:, 0:L], ACT.Relu).then_inc(S["relu_ready"], 1)
                            split_act(act, u.ahead(2))
                            act.wait_ge(S["sq_relu"], i * 4 + at)
                            tile = i * (4 * L) + ((q % 2) * KT + j) * L
                            act.copy(a_hi[:, ds(tile, L)], hbuf[:, (2 + j % 2) * L:(3 + j % 2) * L]).then_inc(S["hi_relu"], 1)
                        elif not isinstance(i, int) or u.c + i * 4 + 2 < N_UNITS:
                            split_act(act, u.ahead(2))
                    run(act, turn_, c + KT == N_UNITS)
                    c += KT

        @block.vector
        def _(dve):
            own = Chain(dve, S["dve_own"])
            tt, ts, stt = dve.tensor_tensor, dve.tensor_scalar, dve.scalar_tensor_tensor

            def conv(pad, acc, n, weight):
                own.link(ts(acc[:, 0:n], pad[:, 0:n], weight(0), None, ALU.mult))
                for k in range(1, TAPS):
                    m = stt(acc[:, 0:n], pad[:, k:k + n], weight(k), acc[:, 0:n], ALU.mult, ALU.add)
                    if k < TAPS - 1:
                        own.link(m)
                return m

            dve.wait_ge(S["c_silu"], 1)
            tt(d3(c4[:], 4)[:, :, 2:4], d3(cs[:], 2), d3(c4[:], 4)[:, :, 0:2], ALU.subtract).then_inc(S["c_ready"], 1)
            dve.wait_ge(S["rel_mm"], 1)
            dve.tensor_copy(by_dist[0:16, :], psum[5][0:16, 0:DIST]).then_inc(S["rel_copy"], 1)
            split_dve_halves(dve, Unit(0))
            split_dve_halves(dve, Unit(1))
            with dve.Fori(0, 12) as i:
                for q in range(4):
                    split_dve_halves(dve, Unit(q + 2, i))
            dve.wait_ge(S["ada_cols"], 12)
            dve.wait_ge(S["xr_ready"], KT)
            own.link(tt(d3(mods[:], 2), d3(psum[3][:, 0:96], 2), bc(par("b_ada", 0, 48), 2), ALU.add))
            own.link(stt(d3(coef[:], 2), d3(mods[:, 32:64], 2), 1.0, bc(par("pre", 0, KT), 2), ALU.add, ALU.mult))

            def low(k):
                dve.wait_ge(S["u_hi"], k + 1)
                tt(a_lo[:, k * T:(k + 1) * T], xr[:, k * T:(k + 1) * T], a_hi[:, k * T:(k + 1) * T],
                   ALU.subtract).then_inc(S["u_ready"], 1)
            for k in range(KT):
                for v in range(2):
                    x = xr[:, k * T + v * L:k * T + (v + 1) * L]
                    m = ts(x, x, coef[:, 2 * k + v:2 * k + v + 1], mods[:, 2 * k + v:2 * k + v + 1], ALU.mult, ALU.add)
                m.then_inc(S["u_f32"], 1)
                if k:
                    low(k - 1)
            low(KT - 1)
            leave(dve, 1)

            dve.wait_ge(unit_done, U_SMALL + 1)
            ts(sm[:], psum[0][:], par("sign"), par("dt_bias"), ALU.mult, ALU.add).then_inc(S["sm_lin"], 1)
            split_dve(dve, Unit(U_SMALL + 2))
            dve.wait_ge(S["sm_soft"], 1)
            own.add(stt(sm[:], sm[:], 0.0, sm_e[:], ALU.max, ALU.add))
            own.link(tt(gmul[:, 1:2], gmul[:, 0:1], par("mul"), ALU.mult))
            ts(sm_e[:], sm[:], gmul[:, 1:2], None, ALU.mult).then_inc(S["sm_mul"], 1)
            dve.wait_ge(S["sm_sums"], 1)
            cum3, tot3, end3, exp3, dec3 = (d3(a[:], 48) for a in (gcum, gtot, gend, gexp, gdec))
            for d in range(2):
                b = d3(psum[3][:, d * 192:d * 192 + 192], 48)
                dve.tensor_copy(cum3[:, :, d * 16:d * 16 + 16], b[:, :, d * 16:d * 16 + 16])
                own.add(dve.tensor_copy(cum3[:, :, 32 + d * 8:40 + d * 8], b[:, :, 32 + d * 8:40 + d * 8]))
            own.link(dve.tensor_copy(gtot[:], psum[4][:, 0:192]))
            tt(gend[:], gtot[:], gcum[:], ALU.subtract).then_inc(S["sm_cum"], 1)
            dve.wait_ge(S["sm_exp"], 1)
            tm3 = d3(tm[:], P)

            def head_cols(kind, k=0):
                return wk_g[:].rearrange("p (h k d c) -> p h k d c", k=6, d=2, c=C)[:, :, kind]

            def by_head(a):
                return a.rearrange("p c (d h) -> p h d c", d=2)

            def tile_cols(kind, d):
                return wk_s[:].rearrange("p (t k d c a) -> p t k d c a", k=5, d=2, c=C, a=2)[:, :, kind, d]

            def by_tile(a, d):
                return a.rearrange("p c (d t a) -> p t d c a", d=2, a=2)[:, :, d]
            for d in range(2):
                for kind, a in ((0, tm3[:, :, 32:48]), (1, cum3[:, :, 32:48]), (2, tm3[:, :, 64:80]), (4, end3[:, :, 32:48]),
                                (5, dec3[:, :, 32:48])):
                    dve.tensor_copy(head_cols(kind)[:, :, d], by_head(a)[:, :, d])
                tt(head_cols(3)[:, :, d], by_head(tm3[:, :, 64:80])[:, :, d], by_head(exp3[:, :, 32:48])[:, :, d], ALU.mult)
                for kind, a in ((0, tm3[:, :, 0:32]), (1, cum3[:, :, 0:32]), (2, tm3[:, :, 96:128]), (4, dec3[:, :, 0:32])):
                    dve.tensor_copy(tile_cols(kind, d), by_tile(a, d))
                tt(tile_cols(3, d), by_tile(tm3[:, :, 96:128], d), by_tile(end3[:, :, 0:32], d), ALU.mult)
            leave(dve, 2)
            dve.memset(g_S[:, 0:P], 0.0).then_inc(S["head_done"], 1)
            dve.memset(g_S[:, P:2 * P], 0.0).then_inc(S["tile_done"], 1)
            dve.memset(g_vn[:, 0:P], 0.0).then_inc(S["s_ready"], 1)
            dve.memset(g_vn[:, P:2 * P], 0.0).then_inc(S["h_ready"], 1)
            dve.wait_ge(S["ld_masks"], 16)

            def col(kind, d, c):
                k = kind * 8 + d * 4 + c
                return g_w[:, k:k + 1]

            def cols4(kind, d):
                return g_w[:, kind * 8 + d * 4:kind * 8 + d * 4 + 4]
            def conv_head(i, h, j):
                dve.wait_ge(S["pad_ready"], i * 3 + (h * 3 + j + 1))
                conv(g_pad[j], g_acc[j], 520 if j else 262,
                     lambda k: par("conv_gdn", i * TAPS + ((j * HG + h) * TAPS + k))).then_inc(S["conv_done"], 1)

            def head(i, more):
                u = Unit(U_GDN, i)
                dve.wait_ge(S["g_rows"], i + 1)
                for d in range(2):
                    for c in range(C):
                        b = (d * 4 + c) * P
                        stt(g_L[:, b:b + P], psum[6 + d][:, c * P:(c + 1) * P], col(1, d, c), K("pos", d), ALU.subtract, ALU.add)
                for d in range(2):
                    for c in range(2):
                        b = (d * 2 + c) * P
                        m = stt(g_A[:, b:b + P], psum[6 + d][:, c * P:(c + 1) * P], col(1, d, c), K("neg", d), ALU.subtract, ALU.add)
                m.then_inc(S["dpre"], 1)
                dve.wait_ge(S["gr_ready"], i + 1)
                tt(g_q[:], g_q[:], g_M[0][:, T:T + L], ALU.mult)
                tt(g_k[:], g_k[:], g_M[0][:, 0:T], ALU.mult).then_inc(S["kn_ready"], 1)
                split_dve(dve, u.ahead(5))
                dve.wait_ge(S["dexp"], i + 1)
                dve.wait_ge(S["gram"], i * 2 + 1)
                for d in range(2):
                    for c in range(C):
                        b = (d * 4 + c) * P
                        m = stt(g_L[:, b:b + P], psum[4][:, c * P:(c + 1) * P], col(2, d, c), g_L[:, b:b + P], ALU.mult, ALU.mult)
                m.then_inc(S["l_ready"], 1)
                dve.wait_ge(S["gram"], i * 2 + 2)
                for d in range(2):
                    tt(g_A[:, d * L:(d + 1) * L], g_A[:, d * L:(d + 1) * L], psum[5][:, 0:L], ALU.mult)
                for d in range(2):
                    m = tt(g_qd[:, d * L:(d + 1) * L], g_qd[:, d * L:(d + 1) * L], g_q[:], ALU.mult)
                m.then_inc(S["aq_ready"], 1)
                for d in range(2):
                    half = slice(d * 512, d * 512 + 512)
                    dve.wait_ge(S["x_mm"], i * 14 + (d + 1))
                    stt(d3(g_U[:, half], P), d3(psum[2 + d][:], P), -1.0, over(IDENT, 4), ALU.mult, ALU.add)
                    m = stt(d3(g_T[:, half], P), d3(g_M[0][:, half], P), -1.0, over(IDENT, 4), ALU.mult, ALU.add)
                m.then_inc(S["first_ut"], 1)
                if more:
                    split_dve(dve, u.ahead(6))
                for level in range(1, LEVELS):
                    for d in range(2):
                        dve.wait_ge(S["x_mm"], i * 14 + (2 * level + d + 1))
                        stt(d3(g_X[:, d * 512:d * 512 + 512], P), d3(psum[4 + d][:], P), -1.0, over(IDENT, 4),
                            ALU.mult, ALU.add).then_inc(S["xp_ready"], 1)
                    if more and level in (3, 5, 6):
                        conv_head(i, 1, (3, 5, 6).index(level))
                    elif more and level == 4:
                        split_dve(dve, u.ahead(7))
                for kind, out, bank, turn_ in ((3, g_kb, 2, 1), (4, g_ke, 2, 1), (2, g_vb, 3, 2)):
                    dve.wait_ge(S["nw_mm"], i * 4 + turn_)
                    for d in range(2):
                        m = tt(d3(out[:, d * 512:d * 512 + 512], P), d3(psum[bank][:], P), bc(cols4(kind, d), P), ALU.mult)
                    if kind != 4:
                        m.then_inc(S["tok_used"], 1)
                for step in range(3):
                    for d in range(2):
                        dve.wait_ge(S["s_mm"], i * 6 + (2 * step + d + 1))
                        s, add = g_S[:, d * P:(d + 1) * P], psum[2 + d][:, 0:P]
                        if step == 0:
                            m = dve.tensor_copy(s, add)
                        else:
                            m = stt(s, s, col(5, d, ORDER[d][step]), add, ALU.mult, ALU.add)
                        m.then_inc(S["s_ready"], 1)
                if more:
                    split_dve(dve, u.ahead(8))
                dve.wait_ge(S["o_rs"], i + 1)
                own.link(stt(g_vn[:], psum[4][:, 0:L], par("gdn_norm"), g_M[0][:, L:2 * L], ALU.mult, ALU.mult))
                z = x_res[:, ds(i * L + HG * L, L)]
                tt(z, z, g_vn[:], ALU.mult).then_inc(S["head_done"], 1)

            for j in range(3):
                split_dve(dve, Unit(U_GDN + j + 2))
                conv_head(0, 0, j)
            with dve.Fori(0, HG - 1) as i:
                own.begin(i, 13)
                head(i, True)
            own.end(HG - 1)
            head(HG - 1, False)

            leave(dve, 3)
            dve.wait_ge(S["pads_set"], 2)
            for j in range(4):
                split_dve(dve, Unit(U_BC + j + 2))
                dve.wait_ge(S["bc_pad"], j + 1)
                if j:
                    dve.wait_ge(S["bc_ready"], j)
                conv(s_pad, s_acc, 520 if j < 2 else 262,
                     lambda k: par("conv_ssd", (8 + j) * TAPS + k)).then_inc(S["bc_conv"], 1)

            def conv_tile(i, t):
                dve.wait_ge(S["sx_pad"], i * 2 + (t + 1))
                conv(s_pad, s_acc, 520, lambda k: par("conv_ssd", i * (2 * TAPS) + (t * TAPS + k))).then_inc(S["sx_conv"], 1)
                split_dve(dve, Unit(U_SSD + 2 * t + 2, i))
            dve.wait_ge(S["bc_ready"], 4)
            conv_tile(0, 0)
            dve.wait_ge(S["bc_tok"], 1)
            for g in range(2):
                def tile(i, t, more):
                    u = Unit(U_SSD + 2 * t, i)
                    dve.wait_ge(S["s_rows"], i * 2 + (t + 1))
                    for d in range(2):
                        for e in range(4):
                            b = (d * 4 + e) * P
                            k = 16 + d * 8 + e
                            m = stt(s_M[:, b:b + P], psum[3 + d][:, e * P:(e + 1) * P], s_w[:, k:k + 1], K("neg", d),
                                    ALU.subtract, ALU.add)
                    m.then_inc(S["s_pre"], 1)
                    split_dve(dve, u.ahead(3))
                    dve.wait_ge(S["s_tok"], i * 2 + (t + 1))
                    for d in range(2):
                        m = tt(d3(s_de[:, d * T:(d + 1) * T], 64), d3(psum[2][:], 64), bc(s_w[:, 48 + d * 8:56 + d * 8], 64), ALU.mult)
                    m.then_inc(S["s_de_ready"], 1)
                    for d in range(2):
                        tt(d3(s_dt[:, d * L:(d + 1) * L], 64), d3(psum[2][:, 0:L], 64), bc(s_w[:, 32 + d * 8:36 + d * 8], 64), ALU.mult)
                    dve.wait_ge(S["st_mm"], i * 2 + (t + 1))
                    for d in range(2):
                        own.add(dve.tensor_copy(s_H[:, d * 3 * P:(d * 3 + 1) * P], psum[5 + d][:, 0:P]))
                    for n in (1, 2):
                        own.wait()
                        for d in range(2):
                            for e in range(2):
                                at = (d * 3 + n) * P + e * 64
                                k = 64 + d * 8 + ORDER[d][n] * 2 + e
                                m = stt(s_H[:, at:at + 64], s_H[:, at - P:at - P + 64], s_w[:, k:k + 1],
                                        psum[5 + d][:, n * P + e * 64:n * P + e * 64 + 64], ALU.mult, ALU.add)
                                if n == 1:
                                    own.add(m)
                    m.then_inc(S["h_ready"], 1)
                    dve.wait_ge(S["s_exp"], i * 2 + (t + 1))

                    def four(ap, d):
                        return ap[:, d * T:(d + 1) * T].rearrange("p (c a q) -> p c a q", c=2, a=2)

                    def pair(ap):
                        return d3(ap, P).unsqueeze(2).broadcast_to([P, 2, 2, P])
                    for d in range(2):
                        tt(four(s_M[:], d), four(s_M[:], d), pair(s_cb[:, g * L:(g + 1) * L]), ALU.mult)
                        m = tt(four(s_C[:], d), four(s_C[:], d), pair(s_ct[:, g * L:(g + 1) * L]), ALU.mult)
                    m.then_inc(S["s_mc_ready"], 1)
                    if more:
                        conv_tile(i, t + 1)
                    dve.wait_ge(S["y_mm"], i * 2 + (t + 1))
                    own.link(stt(s_y[:], s_x[t % 2][:, 0:L], par("skip", i * 2 + t), psum[7][:, 0:L], ALU.mult, ALU.add))
                    z = x_res[:, ds(i * (2 * L) + t * L, L)]
                    tt(z, z, s_y[:], ALU.mult).then_inc(S["tile_done"], 1)
                tiles(dve, g, 2 * 11, tile, own)
                dve.wait_ge(S["grp_rs"], g + 1)
                for k in range(4):
                    x = x_res[:, (g * 4 + k) * L:(g * 4 + k + 1) * L]
                    stt(x, x, par("ssd_norm", g * 4 + k), s_y[:], ALU.mult, ALU.mult)
            leave(dve, 4)

            for q in range(4):
                dve.wait_ge(S["y_hi"], q + 1)
                x = slice(q * 1024, (q + 1) * 1024)
                tt(a_lo[:, x], x_res[:, x], a_hi[:, x], ALU.subtract).then_inc(S["y_ready"], 1)
            lam = d3(par("lam", 0, LAYERS * 4 * DK), DK)
            own.link(tt(d3(b_s[:, 0:4 * DK], DK), lam[:, 0:8:2], lam[:, 1:8:2], ALU.mult))
            dve.tensor_reduce(small[:, 16:20], d3(b_s[:, 0:4 * DK], DK), AX.X, ALU.add).then_inc(S["lam_d"], 1)
            dve.memset(b_cm[:, 0:1], 0.0).then_inc(S["mlp_ready"], 1)
            dve.memset(b_cm[:, 1:2], 0.0).then_inc(S["mlp_ready"], 1)
            own.add(tt(small[:, 0:KT], mods[:, 64:96:2], par("post", 0, KT), ALU.mult))
            for l in range(LAYERS):
                own.add(ts(small[:, 26 + l:27 + l], par("subln", l), 1.0 - lam_init(l), None, ALU.mult))
            with dve.Fori(0, KT // 4) as i:
                for j in range(4):
                    split_dve(dve, Unit(U_WOUT + j + 2, i))
            own.wait()
            dve.wait_ge(S["x_loaded"], 16)
            dve.wait_ge(S["rs_ready"], 1)

            def gated(k):
                own.add(stt(hbuf[:, (k % 4) * L:(k % 4 + 1) * L], mo[:, k * L:(k + 1) * L], small[:, k:k + 1], n_rs[:],
                            ALU.mult, ALU.mult))
            gated(0)
            for k in range(KT):
                own.wait()
                if k + 1 < KT:
                    gated(k + 1)
                x = x_res[:, k * L:(k + 1) * L]
                tt(x, x, hbuf[:, (k % 4) * L:(k % 4 + 1) * L], ALU.add).then_inc(S["sx_upd"], 1)
            dve.wait_ge(S["lam_e"], 1)
            own.link(tt(small[:, 24:26], small[:, 21:24:2], small[:, 20:24:2], ALU.subtract))
            for l in range(LAYERS):
                own.add(ts(small[:, 24 + l:25 + l], small[:, 24 + l:25 + l], -lam_init(l), None, ALU.add))

            def norm(e, name, l):
                dve.wait_ge(S["rs_ready"], e + 2)

                def low(g):
                    dve.wait_ge(S["h_hi_ready"], e * 8 + g + 1)
                    tt(h_lo[:, g * T:(g + 1) * T], hbuf[:, (g % 2) * T:(g % 2) * T + T], h_hi[:, g * T:(g + 1) * T],
                       ALU.subtract).then_inc(S["h_ready2"], 1)
                for g in range(8):
                    if g >= 2:
                        dve.wait_ge(S["h_ready2"], e * 8 + g - 1)
                    for k in range(2 * g, 2 * g + 2):
                        m = stt(hbuf[:, (k % 4) * L:(k % 4 + 1) * L], x_res[:, k * L:(k + 1) * L], par(name, l * KT + k), n_rs[:],
                                ALU.mult, ALU.mult)
                    m.then_inc(S["h_f32"], 1)
                    if g:
                        low(g - 1)
                low(7)

            for l in range(LAYERS):
                base = U_LAYER + l * N_LAYER
                dve.wait_ge(S["sx_upd"], (2 * l + 1) * KT)
                norm(2 * l, "attn_norm", l)
                if l:
                    dve.wait_ge(S["bias_ready"], 16)
                def at(i, j):
                    return i * 2 + (l * HEADS + j + 1)

                def attn_f32(i, j):
                    dve.wait_ge(S["av_rs"], at(i, j))
                    stt(b_o[:], psum[7][:, 0:L], small[:, 26 + l:27 + l], b_or[:], ALU.mult, ALU.mult
                        ).then_inc(S["attn_f32"], 1)

                def attn_low(i, j):
                    dve.wait_ge(S["attn_hi"], at(i, j))
                    y = ds(i * (2 * L) + j * L, L)
                    tt(a_lo[:, y], b_o[:], a_hi[:, y], ALU.subtract).then_inc(S["yt_ready"], 1)

                def head(i, j):
                    last = None if isinstance(i, int) and i + j == 0 else (i, j - 1)
                    u = Unit(base + 6 * j, i, 3)
                    for m in range(3):
                        split_dve(dve, u.ahead(m + 2))
                    dve.wait_ge(S["rs_qk"], at(i, j))
                    for m, name in enumerate(("qg", "kg")):
                        x = b_qk[:, m * L:(m + 1) * L]
                        s = stt(x, x, par(name, l), b_rs[:, m * L:(m + 1) * L], ALU.mult, ALU.mult)
                    s.then_inc(S["qk_ready"], 1)
                    if last:
                        attn_f32(*last)
                    split_dve(dve, u.ahead(5))
                    if last:
                        attn_low(*last)
                    dve.wait_ge(S["score_mm"], at(i, j))
                    b = bias[:, ds(i * (4 * L) + j * 2 * L, 2 * L)]
                    for m in range(2):
                        s = m * 3 * P
                        own.add(stt(b_s[:, s:s + L], psum[3 + m][:, 0:L], DK ** -0.5, b[:, m * L:(m + 1) * L], ALU.mult, ALU.add))
                        own.add(stt(b_s[:, s + L:s + 3 * P], psum[3 + m][:, L:L + P], DK ** -0.5, b[:, m * L + P:(m + 1) * L],
                                    ALU.mult, ALU.add))
                    own.wait()
                    parts = d3(b_s, 3 * P)
                    dve.tensor_reduce(b_st[:, 0:2], parts[:, :, 0:L], AX.X, ALU.max, negate=True)
                    dve.tensor_reduce(b_st[:, 2:4], parts[:, :, L:3 * P], AX.X, ALU.max, negate=True).then_inc(S["sc_ready"], 1)
                    split_dve(dve, u.ahead(6))
                    dve.wait_ge(S["p_exp"], at(i, j))
                    own.link(dve.reciprocal(b_st[:, 8:12], b_st[:, 4:8]))
                    own.add(ts(b_st[:, 9:12:2], b_st[:, 9:12:2], small[:, 24 + l:25 + l], None, ALU.mult))
                    own.add(ts(b_s[:, 0:L], b_s[:, 0:L], b_st[:, 8:9], None, ALU.mult))
                    own.link(ts(b_s[:, L:3 * P], b_s[:, L:3 * P], b_st[:, 10:11], None, ALU.mult))
                    stt(b_s[:, 0:L], b_s[:, 3 * P:3 * P + L], b_st[:, 9:10], b_s[:, 0:L], ALU.mult, ALU.add)
                    stt(b_s[:, L:3 * P], b_s[:, 3 * P + L:6 * P], b_st[:, 11:12], b_s[:, L:3 * P], ALU.mult, ALU.add
                        ).then_inc(S["p_ready"], 1)
                    split_dve(dve, u.ahead(7))
                    dve.wait_ge(S["gates_ready"], at(i, j))
                    w = [par("conv2", i * 6 + ((l * HEADS + j) * 3 + k)) for k in range(3)]
                    own.link(tt(b_cm[:, 2:2 + L], b_gc[:], b_ci[:], ALU.mult))
                    own.link(ts(b_co[:], b_cm[:, 2:2 + L], w[2], None, ALU.mult))
                    own.link(stt(b_co[:], b_cm[:, 1:1 + L], w[1], b_co[:], ALU.mult, ALU.add))
                    own.link(stt(b_co[:], b_cm[:, 0:L], w[0], b_co[:], ALU.mult, ALU.add))
                    tt(b_co[:], b_co[:], b_gb[:], ALU.mult).then_inc(S["conv_f32"], 1)
                    tile = i * (2 * L) + j * L
                    dve.wait_ge(S["conv_hi"], at(i, j))
                    y = ds(tile + HEADS * L, L)
                    tt(a_lo[:, y], b_co[:], a_hi[:, y], ALU.subtract).then_inc(S["yt_ready"], 1)
                pairs(dve, head, 2 * 12, own)
                attn_f32(HEADS // 2 - 1, 1)
                attn_low(HEADS // 2 - 1, 1)

                def add_to_x(i, c, j, signal):
                    u = Unit(c + j, i)
                    dve.wait_ge(unit_done, u.n + 1)
                    x = x_res[:, ds(i * (4 * L) + j * L, L)]
                    m = tt(x, x, psum[u.bank][:, 0:L], ALU.add)
                    if signal:
                        m.then_inc(S[signal], 1)
                    if not isinstance(i, int) or u.c + i * 4 + 2 < N_UNITS:
                        split_dve(dve, u.ahead(2))
                with dve.Fori(0, KT // 4) as i:
                    for j in range(4):
                        add_to_x(i, base + N_IN2, j, "sx_upd")
                dve.wait_ge(S["sx_upd"], (2 * l + 2) * KT)
                norm(2 * l + 1, "mlp_norm", l)
                c = base + N_IN2 + KT
                for kind, q in MLP_ORDER:
                    def turn_(i, j):
                        if kind == "up":
                            u = Unit(c + j, i)
                            split_dve(dve, u.ahead(2))
                            dve.wait_ge(S["hi_relu"], i * 4 + ((l * FQ + q) * KT + j + 1))
                            tile = ds(i * (4 * L) + ((q % 2) * KT + j) * L, L)
                            tt(a_lo[:, tile], hbuf[:, (2 + j % 2) * L:(3 + j % 2) * L], a_hi[:, tile], ALU.subtract
                               ).then_inc(S["mlp_ready"], 1)
                        else:
                            add_to_x(i, c, j, None if q < 3 else "sx_upd" if l + 1 < LAYERS else "x_final")
                    run(dve, turn_, c + KT == N_UNITS)
                    c += KT


def lam_init(l):
    return 0.8 - 0.6 * math.exp(-0.3 * l)


def run(eng, turn, last):
    with eng.Fori(0, 3 if last else 4) as i:
        for j in range(4):
            turn(i, j)
    if last:
        for j in range(4):
            turn(3, j)


def columns(w):
    n = w.shape[1] // P
    return w.reshape(KT, P, n, P).transpose(2, 1, 0, 3).reshape(n, P, D)


def kernel(**inputs):
    import concourse.bacc as bacc
    from concourse.bass_utils import run_bass_kernel_spmd

    a = {k: np.ascontiguousarray(v) for k, v in inputs.items()}
    w_in, w_ada = a["w_in"][0], a["w_ada"][0]
    xbc, dt = 2048, 2048 + 1536
    qkv = dt + 32
    beta = qkv + 3072
    alpha = beta + 16
    none = np.zeros((D, 16), np.float32)
    small = np.concatenate([w_in[:, dt:qkv], w_in[:, alpha:alpha + 16], none, w_in[:, beta:beta + 16], none,
                            w_in[:, dt:qkv]], axis=1)
    z, x, bc = columns(w_in[:, 0:2048]), columns(w_in[:, xbc:xbc + 1024]), columns(w_in[:, xbc + 1024:dt])
    qkv_u = columns(w_in[:, qkv:beta])
    parts = [w_ada.reshape(4, 4, P, 12, 512).transpose(3, 0, 2, 1, 4).reshape(48, P, D), columns(small)]
    parts += [np.stack([qkv_u[h], qkv_u[HG + h], qkv_u[2 * HG + h], z[TS + h]]) for h in range(HG)]
    parts += [bc]
    parts += [np.stack([x[t], z[t]]) for t in range(TS)]
    parts += [columns(a["w_out"][0])]
    for l in range(LAYERS):
        w2 = columns(a["w_in_2"][l])
        parts += [w2[[h + 8 * k for k in range(6)]] for h in range(HEADS)]
        parts += [columns(a["w_out_2"][l])]
        for kind, q in MLP_ORDER:
            if kind == "up":
                parts += [columns(a["w_up_2"][l][:, q * D:(q + 1) * D])]
            else:
                parts += [columns(a["w_down_2"][l][q * D:(q + 1) * D])]
    stream = np.concatenate(parts)
    assert stream.shape == (N_UNITS, P, D)

    def feat(v):
        return np.ascontiguousarray(v.reshape(-1, P).T)

    pars = np.zeros((P, N_PAR), np.float32)

    def par(name, v):
        at, w = PAR[name]
        assert v.shape == (P, w), (name, v.shape)
        pars[:, at:at + w] = v
    par("c", np.stack([a["c"].reshape(KT, P).T, a["c_ctx"].reshape(KT, P).T], axis=2).reshape(P, 2 * KT))
    par("b_ada", feat(a["b_ada"]))
    par("pre", feat(a["pre_norm_w"]))
    par("post", feat(a["post_norm_w"]))
    par("conv_ssd", a["conv_ssd_w"].reshape(TAPS, 12, P).transpose(2, 1, 0).reshape(P, -1))
    par("bias_ssd", feat(a["conv_ssd_b"]))
    par("conv_gdn", a["conv_gdn_w"].reshape(TAPS, 24, P).transpose(2, 1, 0).reshape(P, -1))
    rows = np.zeros((4, P), np.float32)
    rows[0] = 1.0
    rows[0, 64:96] = -1.0
    rows[1, 0:32] = rows[1, 96:128] = a["ssd_dt_bias"].reshape(-1)
    rows[1, 32:48] = a["gdn_dt_bias"].reshape(-1)
    rows[2, 0:32] = a["ssd_a_log"].reshape(-1)
    rows[2, 32:48] = a["gdn_a_log"].reshape(-1)
    rows[3] = 1.0
    rows[3, 0:48] = -1.0
    for k, name in enumerate(("sign", "dt_bias", "a_log", "mul")):
        par(name, rows[k][:, None])
    par("skip", feat(np.repeat(a["ssd_d"].reshape(-1), 64)))
    par("ssd_norm", feat(a["ssd_norm_w"]))
    par("gdn_norm", feat(a["gdn_norm_w"]))
    par("attn_norm", feat(a["attn_norm_g_2"]))
    par("mlp_norm", feat(a["mlp_norm_g_2"]))
    par("conv2", a["conv_w_2"].reshape(LAYERS, 3, HEADS, P).transpose(3, 0, 2, 1).reshape(P, -1))
    par("qg", np.tile(a["q_norm_g_2"], (1, 2)).T)
    par("kg", np.tile(a["k_norm_g_2"], (1, 2)).T)
    par("subln", a["subln_g_2"].T)
    lam = np.stack([a[f"lambda_{n}_2"] for n in ("q1", "k1", "q2", "k2")], axis=1)
    par("lam", np.broadcast_to(lam.reshape(1, -1), (P, lam.size)))
    x_t = np.ascontiguousarray(np.concatenate([a["x"][0], a["ctx"][0]]).T)

    nc = bacc.Bacc("TRN2", target_bir_lowering=False, num_devices=1)
    arrays = {"stream": stream, "x_t": x_t, "const": constants(), "buckets": bucket_rows(), "pars": pars, "rel": a["rel_bias_2"]}
    handles = [nc.dram_tensor(k, v.shape, F32, kind="ExternalInput").ap() for k, v in arrays.items()]
    out = nc.dram_tensor("out_t", (D, L), F32, kind="ExternalOutput").ap()
    scratch = [nc.dram_tensor("by_distance", (2 * HEADS, DIST), F32, kind="Internal").ap(),
               nc.dram_tensor("bias_table", (P, 2 * HEADS * L), F32, kind="Internal").ap()]
    build(nc, *handles, out, scratch)
    r = run_bass_kernel_spmd(nc, [arrays], core_ids=[0])
    return np.ascontiguousarray(r.results[0]["out_t"].T).reshape(1, L, D)
```
